# Optimizing a Trainium2 kernel written in Bass

```python
import jax, jax.numpy as jnp
from jax import lax
import numpy as np

D_MODEL = 1024
BATCH = 1
SEQ = 1024
DEPTH = 1

CHUNK = 64
N_META = 16
HEAD_DIM = 64
SB_HEADS = 8
SWA_HEADS = 8
SWA_KV_HEADS = 2
SWA_GROUP = SWA_HEADS // SWA_KV_HEADS
SB_WIDTH = SB_HEADS * HEAD_DIM
SWA_WIDTH = SWA_HEADS * HEAD_DIM
SWA_KV_WIDTH = SWA_KV_HEADS * HEAD_DIM
MIX_WIDTH = SB_WIDTH + SWA_WIDTH
IN_WIDTH = 3 * SB_WIDTH + SWA_WIDTH + 2 * SWA_KV_WIDTH
IN_SPLITS = (SB_WIDTH, 2 * SB_WIDTH, 3 * SB_WIDTH, 3 * SB_WIDTH + SWA_WIDTH,
             3 * SB_WIDTH + SWA_WIDTH + SWA_KV_WIDTH)
SB_BLOCK = 128
WINDOW = 128
WINDOW_CHUNKS = WINDOW // CHUNK
ROPE_THETA = 10000.0
PEER_HEADS = 8
PEER_N_KEYS = 128
PEER_N_EXPERTS = PEER_N_KEYS * PEER_N_KEYS
PEER_KEY_DIM = 128
PEER_HALF = PEER_KEY_DIM // 2
PEER_TOPK = 16
PEER_TOKEN_BLOCK = 128
RMS_EPS = 1e-6

kernel_name = 'hybrid_stickbreak_swa_sink_peer_block'

def rmsnorm(x, gain):
    xf = x.astype(jnp.float32)
    y = xf * lax.rsqrt(jnp.mean(xf * xf, axis=-1, keepdims=True) + RMS_EPS)
    return (y * gain.astype(jnp.float32)).astype(x.dtype)

def rope(x, pos):
    half = HEAD_DIM // 2
    inv_freq = ROPE_THETA ** (-jnp.arange(half, dtype=jnp.float32) / half)
    ang = pos.astype(jnp.float32)[:, None] * inv_freq[None, :]
    cos = jnp.cos(ang)[None, :, None, :]
    sin = jnp.sin(ang)[None, :, None, :]
    xf = x.astype(jnp.float32)
    x1, x2 = xf[..., :half], xf[..., half:]
    return jnp.concatenate([x1 * cos - x2 * sin, x2 * cos + x1 * sin], axis=-1).astype(x.dtype)

def stick_breaking_attention(q, k, v):
    L = q.shape[2]
    n_blk = -(-L // SB_BLOCK)
    pad = n_blk * SB_BLOCK - L
    padw = ((0, 0), (0, 0), (0, pad), (0, 0))
    q, k, v = jnp.pad(q, padw), jnp.pad(k, padw), jnp.pad(v, padw)
    scale = HEAD_DIM ** -0.5
    outs = []
    for i in range(n_blk):
        kv_len = (i + 1) * SB_BLOCK
        q_i = q[:, :, i * SB_BLOCK:kv_len]
        k_i, v_i = k[:, :, :kv_len], v[:, :, :kv_len]
        z = jnp.einsum('bhqd,bhkd->bhqk', q_i, k_i).astype(jnp.float32) * scale
        t_idx = i * SB_BLOCK + jnp.arange(SB_BLOCK)
        s_idx = jnp.arange(kv_len)
        mask = s_idx[None, :] < t_idx[:, None]
        log_fail = jnp.where(mask, -jax.nn.softplus(z), 0.0)
        later_fail = lax.cumsum(log_fail, axis=3, reverse=True) - log_fail
        w = jnp.where(mask, jnp.exp(jax.nn.log_sigmoid(z) + later_fail), 0.0)
        outs.append(jnp.einsum('bhqk,bhkd->bhqd', w.astype(v.dtype), v_i))
    return jnp.concatenate(outs, axis=2)[:, :, :L]

def _sink_attend(qx, kx, vx, mask, sink):
    s = jnp.einsum('bcqkgd,bcskd->bckgqs', qx, kx).astype(jnp.float32) * (HEAD_DIM ** -0.5)
    s = jnp.where(mask[None, :, None, None, None, :], s, -jnp.inf)
    sk = jnp.broadcast_to(sink[None, None, :, :, None, None], s.shape[:-1] + (1,))
    p = jax.nn.softmax(jnp.concatenate([s, sk], axis=-1), axis=-1)[..., :-1]
    return jnp.einsum('bckgqs,bcskd->bcqkgd', p.astype(vx.dtype), vx)

def sliding_window_sink_attention(q, k, v, sinks):
    B, L = q.shape[0], q.shape[1]
    n_real = L - N_META
    nc = n_real // CHUNK
    n_prev = WINDOW_CHUNKS - 1
    sink = sinks.astype(jnp.float32).reshape(SWA_KV_HEADS, SWA_GROUP)
    qg = q.reshape(B, L, SWA_KV_HEADS, SWA_GROUP, HEAD_DIM)
    o_meta = _sink_attend(qg[:, None, :N_META], k[:, None, :N_META], v[:, None, :N_META],
                          jnp.ones((1, N_META), dtype=bool), sink)
    o_meta = o_meta.reshape(B, N_META, SWA_WIDTH)
    qr = qg[:, N_META:].reshape(B, nc, CHUNK, SWA_KV_HEADS, SWA_GROUP, HEAD_DIM)

    def band(t):
        tc = t[:, N_META:].reshape(B, nc, CHUNK, SWA_KV_HEADS, HEAD_DIM)
        tp = jnp.pad(tc, ((0, 0), (n_prev, 0), (0, 0), (0, 0), (0, 0)))
        win = jnp.concatenate([tp[:, j:j + nc] for j in range(WINDOW_CHUNKS)], axis=2)
        meta = jnp.broadcast_to(t[:, None, :N_META], (B, nc, N_META, SWA_KV_HEADS, HEAD_DIM))
        return jnp.concatenate([meta, win], axis=2)

    offset = jnp.repeat(jnp.arange(WINDOW_CHUNKS) - n_prev, CHUNK)
    valid = (jnp.arange(nc)[:, None] + offset[None, :]) >= 0
    mask = jnp.concatenate([jnp.ones((nc, N_META), dtype=bool), valid], axis=1)
    o_real = _sink_attend(qr, band(k), band(v), mask, sink).reshape(B, n_real, SWA_WIDTH)
    return jnp.concatenate([o_meta, o_real], axis=1)

def hybrid_mixer(h, ln, w_in, sb_norm, swa_norm, sinks, w_out):
    B, L = h.shape[0], h.shape[1]
    xn = rmsnorm(h, ln)
    proj = xn @ w_in
    qa, ka, va, qb, kb, vb = jnp.split(proj, IN_SPLITS, axis=-1)
    heads_a = lambda t: t.reshape(B, L, SB_HEADS, HEAD_DIM).transpose(0, 2, 1, 3)
    o_a = stick_breaking_attention(heads_a(qa), heads_a(ka), heads_a(va))
    o_a = o_a.transpose(0, 2, 1, 3).reshape(B, L, SB_WIDTH)
    pos = jnp.arange(L)
    qb = rope(qb.reshape(B, L, SWA_HEADS, HEAD_DIM), pos)
    kb = rope(kb.reshape(B, L, SWA_KV_HEADS, HEAD_DIM), pos)
    vb = vb.reshape(B, L, SWA_KV_HEADS, HEAD_DIM)
    o_b = sliding_window_sink_attention(qb, kb, vb, sinks)
    o = jnp.concatenate([rmsnorm(o_a, sb_norm), rmsnorm(o_b, swa_norm)], axis=-1)
    return o @ w_out

def peer_ffn(x, w_query, sub_keys, expert_u, expert_v):
    B, S, D = x.shape
    T = B * S
    n_blk = -(-T // PEER_TOKEN_BLOCK)
    t = jnp.pad(x.reshape(T, D), ((0, n_blk * PEER_TOKEN_BLOCK - T), (0, 0)))
    t = t.reshape(n_blk, PEER_TOKEN_BLOCK, D)

    def block(tb):
        q = (tb @ w_query).reshape(PEER_TOKEN_BLOCK, PEER_HEADS, 2, PEER_HALF)
        s = jnp.einsum('thpd,hpnd->thpn', q, sub_keys)
        s1, i1 = lax.top_k(s[:, :, 0], PEER_TOPK)
        s2, i2 = lax.top_k(s[:, :, 1], PEER_TOPK)
        cand_s = (s1[..., :, None] + s2[..., None, :]).reshape(PEER_TOKEN_BLOCK, PEER_HEADS, PEER_TOPK * PEER_TOPK)
        cand_i = (i1[..., :, None] * PEER_N_KEYS + i2[..., None, :]).reshape(PEER_TOKEN_BLOCK, PEER_HEADS, PEER_TOPK * PEER_TOPK)
        top_s, pos = lax.top_k(cand_s, PEER_TOPK)
        idx = jnp.take_along_axis(cand_i, pos, axis=-1)
        g = jax.nn.softmax(top_s.astype(jnp.float32), axis=-1)
        u = expert_u[idx]
        act = jax.nn.gelu(jnp.einsum('thkd,td->thk', u, tb).astype(jnp.float32), approximate=False)
        coef = (g * act).astype(tb.dtype)
        return jnp.einsum('thk,thkd->td', coef, expert_v[idx])

    out = lax.map(block, t).reshape(n_blk * PEER_TOKEN_BLOCK, D)[:T]
    return out.reshape(B, S, D)

def setup_inputs(seed: int = 0) -> dict:
    key = jax.random.key(seed)
    ks = jax.random.split(key, 16)
    f32 = jnp.float32
    nrm = lambda k, shape, s: jax.random.normal(k, shape, f32) * s
    return {
        'x': nrm(ks[0], (BATCH, SEQ, D_MODEL), 1.0),
        'meta_tokens': nrm(ks[1], (N_META, D_MODEL), 1.0),
        'ln_mix': 1.0 + nrm(ks[2], (DEPTH, D_MODEL), 0.02),
        'w_in': nrm(ks[3], (DEPTH, D_MODEL, IN_WIDTH), D_MODEL ** -0.5),
        'sb_out_norm': 1.0 + nrm(ks[4], (DEPTH, SB_WIDTH), 0.02),
        'swa_out_norm': 1.0 + nrm(ks[5], (DEPTH, SWA_WIDTH), 0.02),
        'sinks': nrm(ks[6], (DEPTH, SWA_HEADS), 0.5),
        'w_out': nrm(ks[7], (DEPTH, MIX_WIDTH, D_MODEL), MIX_WIDTH ** -0.5),
        'ln_ffn': 1.0 + nrm(ks[8], (DEPTH, D_MODEL), 0.02),
        'peer_query': nrm(ks[9], (DEPTH, D_MODEL, PEER_HEADS * PEER_KEY_DIM), D_MODEL ** -0.5),
        'peer_sub_keys': nrm(ks[10], (DEPTH, PEER_HEADS, 2, PEER_N_KEYS, PEER_HALF), PEER_HALF ** -0.5),
        'expert_u': nrm(ks[11], (DEPTH, PEER_N_EXPERTS, D_MODEL), D_MODEL ** -0.5),
        'expert_v': nrm(ks[12], (DEPTH, PEER_N_EXPERTS, D_MODEL), 0.1),
        'final_norm': 1.0 + nrm(ks[13], (D_MODEL,), 0.02),
    }

def reference(x, meta_tokens, ln_mix, w_in, sb_out_norm, swa_out_norm, sinks, w_out,
              ln_ffn, peer_query, peer_sub_keys, expert_u, expert_v, final_norm):
    b = x.shape[0]
    meta = jnp.broadcast_to(meta_tokens.astype(x.dtype)[None], (b, N_META, D_MODEL))
    h = jnp.concatenate([meta, x], axis=1)
    for layer in range(DEPTH):
        h = h + hybrid_mixer(h, ln_mix[layer], w_in[layer], sb_out_norm[layer],
                             swa_out_norm[layer], sinks[layer], w_out[layer])
        if layer == DEPTH - 1:
            h = h[:, N_META:]
        h = h + peer_ffn(rmsnorm(h, ln_ffn[layer]), peer_query[layer], peer_sub_keys[layer],
                         expert_u[layer], expert_v[layer])
    return rmsnorm(h, final_norm)


_drawn_inputs = setup_inputs


def setup_inputs(seed=0):
    import zlib

    import numpy as np

    out = dict(_drawn_inputs(seed))
    spreads = {}
    factors = {'sb_out_norm': 17.387,
     'swa_out_norm': 16.875,
     'sinks': 8.0,
     'ln_ffn': 30.244,
     'final_norm': 7.559}
    for name, (base, spread) in spreads.items():
        noise = np.random.default_rng([zlib.crc32(name.encode()), seed]).standard_normal(out[name].shape)
        drawn = base * np.exp(spread * noise) if base else spread * noise
        out[name] = __import__('jax').numpy.asarray(drawn.astype(out[name].dtype))
    for name, factor in factors.items():
        out[name] = (out[name] * factor).astype(out[name].dtype)
    return out
```

```python
from contextlib import ExitStack

import numpy as np

import concourse.bass as bass
from concourse import mybir

F32 = mybir.dt.float32
U32 = mybir.dt.uint32
ALU = mybir.AluOpType
ACT = mybir.ActivationFunctionType
AX = mybir.AxisListType

P = 128
D = 1024
SEQ = 1024
META = 16
HD = 64
HEADS = 8
PAIRS = HEADS // 2
DC = D // P
NT = SEQ // P
L = SEQ + META
QKW = 3 * P
VW = HEADS * HD + P
CHUNK = 64
WIN = META + 3 * CHUNK
PREV = META + CHUNK
KCOLS = META + CHUNK + SEQ
EPS = 1e-6
QSCALE = HD ** -0.5
NKEYS = 128
NEXP = NKEYS * NKEYS
TOPK = 16
PH = 8
K = PH * TOPK
NEG = -1e30
NB = 8
GRP = 2
NG = K // GRP
SEGS = []
_at = 0
for _a0, _na in ((0, 1), (1, 1), (2, 1), (3, 1), (4, 1), (5, 3), (8, 8)):
    _nb = TOPK // (_a0 + 1)
    SEGS.append((_a0, _na, _nb, _at))
    _at += _na * _nb
NC = _at

UNITS = []
for _j in list(range(NT - 1, -1, -1)) + [NT]:
    _t = P * _j if _j < NT else 0
    while _t < SEQ:
        _w = min(512 - _t % 512, SEQ - _t)
        UNITS += [(_j, _t, _w, 0), (_j, _t, _w, 1)]
        _t += _w
NU = len(UNITS)
NADD = sum(u[0] < NT for u in UNITS)
SPANS = ((0, 512), (512, 512), (SEQ, META))
KEY_BANKS = (2, 3, 6, 7)
AHEAD = 2
ZB = 4
assert NU % ZB == 0 and NU % 2 == 0
SPB = 4

C_ID, C_TRI, C_ONES, C_M01, C_MNEG, C_PERM = (P * i for i in range(6))
C_IOTA = 6 * P
C_WM = C_IOTA + NC
C_GAIN = C_WM + 2 * WIN
C_LNM = C_GAIN + 8
C_ALL = C_LNM + DC


class Own:

    def __init__(self, engine, semaphore):
        self.engine, self.semaphore, self.n = engine, semaphore, 0

    def link(self, instruction):
        self.n += 1
        instruction.then_inc(self.semaphore, 1)
        self.engine.wait_ge(self.semaphore, self.n)

    def settle(self):
        if self.n:
            self.engine.wait_ge(self.semaphore, self.n)
            self.engine.sem_clear(self.semaphore)
            self.n = 0


def block_program(nc, x, meta, w_pair, w_v, w_kb, consts, rope_cs, w_out, sinks, ln_ffn, fnorm,
                  w_query, keys_t, experts, out):
    with ExitStack() as ctx:
        def sb(name, words):
            return ctx.enter_context(nc.sbuf_tensor(name, [P, words], F32))

        def sem(name):
            return ctx.enter_context(nc.semaphore(name))

        def scratch(name, shape):
            return nc.dram_tensor(name, shape, F32, kind="Internal").ap()

        def parts(region, sizes):
            at, views = 0, []
            for words in sizes:
                views.append(region[:, at:at + words])
                at += words
            return views

        def grid(view, a):
            return view.rearrange("p (a n) -> p a n", a=a)

        ps = ctx.enter_context(nc.psum_tensor("ps", [P, 8, 512], F32))

        cst = sb("cst", C_ALL)
        ident = cst[:, C_ID:C_ID + P]
        negtri = cst[:, C_TRI:C_TRI + P]
        negones = cst[:, C_ONES:C_ONES + P]
        mask01 = cst[:, C_M01:C_M01 + P]
        maskneg = cst[:, C_MNEG:C_MNEG + P]
        perm = cst[:, C_PERM:C_PERM + P]
        iota = cst[:, C_IOTA:C_IOTA + NC]
        winmask = grid(cst[:, C_WM:C_WM + 2 * WIN], 2)
        mixgain = cst[:, C_GAIN:C_GAIN + 8]
        lnmix = cst[:, C_LNM:C_LNM + DC]
        sinkb = sb("sinkb", HEADS)
        lnb = sb("lnb", D)
        fnb = sb("fnb", D)
        keysT = grid(sb("keysT", PH * NKEYS), PH)

        r_uv = sb("r_uv", NB * 2 * D)
        uv = grid(r_uv[:, :], NB)
        xnT_v, vall_v, xt_v = parts(r_uv, [DC * L, (NT + 1) * VW, 2 * D])
        xnT, vall, xt = grid(xnT_v, DC), grid(vall_v, NT + 1), grid(xt_v, 2)
        r_wo = sb("r_wo", DC * D)
        wout = grid(r_wo[:, :], DC)
        wpair_v, wkb_v, xTc_v, vpair_v = parts(r_wo, [DC * QKW, DC * P, 2 * D, (NT + 1) * P])
        wpair, wkb = grid(wpair_v, DC), grid(wkb_v, DC)
        xTc = xTc_v.rearrange("p (u c n) -> p u c n", u=2, c=DC)
        vpair = grid(vpair_v, NT + 1)
        r_wq = sb("r_wq", DC * D)
        wq = grid(r_wq[:, :], DC)
        wv_v, cos, sin = parts(r_wq, [DC * VW, L, L])
        wv = grid(wv_v, DC)

        hncur = sb("hncur", D)
        h2cur = sb("h2cur", D)
        vprev = sb("vprev", P)
        kbcur = sb("kbcur", WIN)
        small = sb("small", 64)
        r_wk = sb("r_wk", 13104)
        (pT_v, ssb_v, sq_v, qT_v, hs, hnn, qb_v, vown, oa_v, topv_v, topi_v, topf_v, cs_v, ci_v,
         cs2_v, tops_v, pos_v, posf_v, idxf, idxn, gn, actv, gel, idxcur, gcur, diag_v) = parts(r_wk, [
             2048, 2048, D, D, D, D, 512, P, 512, 256, 256, 256, PH * NC, PH * NC,
             PH * NC, K, K, K, K, K, K, K, K, K, K, 4 * P])
        pT = pT_v.rearrange("p (a h n) -> p a h n", a=2, h=8)
        s_all = grid(pT_v, 2 * PH)
        s_tmp = grid(ssb_v, 2 * PH)
        ssb = grid(ssb_v[:, 0:HEADS * WIN], HEADS)
        sq = grid(sq_v, 8)
        hnT = grid(sq_v, DC)
        eq = grid(sq_v[:, 0:TOPK * NC], TOPK)
        qT = grid(qT_v, PH)
        ob = grid(qT_v[:, 0:512], 4)
        qb = grid(qb_v, 4)
        oa = grid(oa_v, 4)
        topv, topf = grid(topv_v, 16), grid(topf_v, 16)
        topi = grid(topi_v.bitcast(U32), 16)
        cs, ci, cs2 = grid(cs_v, PH), grid(ci_v, PH), grid(cs2_v, PH)
        tops, posf = grid(tops_v, PH), grid(posf_v, PH)
        pos = grid(pos_v.bitcast(U32), PH)
        idxf3, gn3, gcur3 = grid(idxf, PH), grid(gn, PH), grid(gcur, PH)
        idxn_u, idxcur_u = idxn.bitcast(U32), idxcur.bitcast(U32)
        diag = grid(diag_v, 4)
        (qpair, kpair, ropx, ropt, az_v, sp_v, w_v2, acc_v, oT) = parts(r_wk, [
            SEQ, L, L, L, 2 * 512, SPB * 512, 2 * 512, 2 * SEQ, SEQ])
        az, sp, wb, acc = grid(az_v, 2), grid(sp_v, SPB), grid(w_v2, 2), grid(acc_v, 2)

        nssq, nr = small[:, 0:2], small[:, 2:4]
        mx, nmx, se, rs, rden = (small[:, 4 + 8 * i:12 + 8 * i] for i in range(5))
        r2 = small[:, 44:46]
        r3 = small[:, 46:48]
        r4 = small[:, 48:50]
        gsum = small[:, 50:58]
        onecol = small[:, 58:59]
        epscol = small[:, 59:60]
        newton = small[:, 60:64]

        qb_dram = scratch("qb_dram", [P, PAIRS, SEQ])
        kb_dram = scratch("kb_dram", [P, KCOLS])
        vb_dram = scratch("vb_dram", [CHUNK + SEQ, P])
        oa_dram = scratch("oa_dram", [P, PAIRS, SEQ])

        consts_in, side_in, wv_in, wkb_in = sem("consts_in"), sem("side_in"), sem("wv_in"), sem("wkb_in")
        x_in = [sem("x_in0"), sem("x_in1")]
        squared, scaled, turned, xT_ready = sem("squared"), sem("scaled"), sem("turned"), sem("xT_ready")
        xT_kept, v_summed, v_kept = sem("xT_kept"), sem("v_summed"), sem("v_kept")
        zeroed, k_summed, k_kept, k_turned, k_roped = (
            sem("zeroed"), sem("k_summed"), sem("k_kept"), sem("k_turned"), sem("k_roped"))
        side_out = sem("side_out")
        wpair_in, proj_summed, proj_kept, q_turned, q_roped = (
            sem("wpair_in"), sem("proj_summed"), sem("proj_kept"), sem("q_turned"), sem("q_roped"))
        vpair_ready, qb_out, qb_free, oa_out, oT_free, oT_ready = (
            sem("vpair_ready"), sem("qb_out"), sem("qb_free"), sem("oa_out"), sem("oT_free"),
            sem("oT_ready"))
        z_ready, abs_ready, log_ready, sp_ready, tri_done, acc_ready, w_ready, w_used = (
            sem("z_ready"), sem("abs_ready"), sem("log_ready"), sem("sp_ready"), sem("tri_done"),
            sem("acc_ready"), sem("w_ready"), sem("w_used"))
        eps_set = sem("eps_set")
        wout_in, wq_in = sem("wout_in"), sem("wq_in")
        wout_scaled = sem("wout_scaled")
        tile_in, score_done, max_ready, exp_ready, p_ready = (
            sem("tile_in"), sem("score_done"), sem("max_ready"), sem("exp_ready"), sem("p_ready"))
        pt_done, pt_kept_a, pt_kept_v, ob_done, ob_ready, ssq_done, r2_ready = (
            sem("pt_done"), sem("pt_kept_a"), sem("pt_kept_v"), sem("ob_done"), sem("ob_ready"),
            sem("ssq_done"), sem("r2_ready"))
        mix_done, h2_ready, h2_squared, hn_ready = (
            sem("mix_done"), sem("h2_ready"), sem("h2_squared"), sem("hn_ready"))
        hnT_done, hnT_kept, qT_done, qT_kept, key_done, key_kept = (
            sem("hnT_done"), sem("hnT_kept"), sem("qT_done"), sem("qT_kept"), sem("key_done"),
            sem("key_kept"))
        gate_in, gate_exp, routed = sem("gate_in"), sem("gate_exp"), sem("routed")
        head_ready, head_in, head_exp = sem("head_ready"), sem("head_in"), sem("head_exp")
        rows_in = [sem(f"rows_in{i}") for i in range(NB)]
        idx_ready, dotted, gelu_ready, diag_ready, rows_used = (
            sem("idx_ready"), sem("dotted"), sem("gelu_ready"), sem("diag_ready"), sem("rows_used"))
        h2_copied, h2_free, h3_ready, h3_squared, out_ready, out_done = (
            sem("h2_copied"), sem("h2_free"), sem("h3_ready"), sem("h3_squared"), sem("out_ready"),
            sem("out_done"))
        passed = {}
        for name in ("pe", "act", "dve", "pool", "sp"):
            passed[name] = sem("passed_" + name)

        act_own, dve_own = sem("act_own"), sem("dve_own")

        def gate(eng, name, semaphore, value):
            eng.wait_ge(semaphore, value)
            eng.sem_inc(passed[name], 1)

        N_SIDE = 4
        block = ctx.enter_context(nc.Block())

        @block.sync
        def _(sp_eng):
            e = sp_eng
            e.dma_start(cst[:, :], consts).then_inc(consts_in, 16)
            e.dma_start(xt[:, 0, :], x[0:P, :]).then_inc(x_in[0], 16)
            e.dma_start(xt[:, 1, :], x[P:2 * P, :]).then_inc(x_in[1], 16)
            e.dma_start(wv[:, :, :], w_v).then_inc(wv_in, 16)
            e.dma_start(wkb[:, :, :], w_kb).then_inc(wkb_in, 16)
            e.dma_start(r_wq[:, DC * VW:DC * VW + 2 * L], rope_cs).then_inc(wkb_in, 16)
            e.dma_start(wpair[:, :, :], w_pair[0]).then_inc(wpair_in, 16)
            with nc.sync.Fori(1, NT // 2) as m:
                for u in range(2):
                    e.wait_ge(turned, 2 * m + u - 1)
                    e.dma_start(xt[:, u, :], x[bass.ds((2 * m + u) * P, P), :]).then_inc(x_in[u], 16)
            e.wait_ge(turned, NT - 1)
            e.dma_start(xt[0:META, 0, :], meta).then_inc(x_in[0], 16)
            e.dma_start(sinkb[:, :], sinks.partition_broadcast(P)).then_inc(side_in, 16)
            e.dma_start(lnb[:, :], ln_ffn.partition_broadcast(P)).then_inc(side_in, 16)
            e.dma_start(fnb[:, :], fnorm.partition_broadcast(P)).then_inc(side_in, 16)
            e.dma_start(keysT[:, :, :], keys_t).then_inc(side_in, 16)
            e.wait_ge(zeroed, 1)
            e.dma_start(vb_dram[0:CHUNK, :], oT[0:CHUNK, 0:P]).then_inc(side_out, 16)
            e.dma_start(kb_dram[:, META:META + CHUNK], oT[:, 0:CHUNK]).then_inc(side_out, 16)
            e.wait_ge(v_kept, NT + 1 + AHEAD)
            e.dma_start(vb_dram[CHUNK:CHUNK + SEQ, :].rearrange("(n p) c -> p n c", p=P),
                        vall[:, 0:NT, HEADS * HD:VW]).then_inc(side_out, 16)
            e.dma_start(vprev[0:META, :], vall[0:META, NT, HEADS * HD:VW]).then_inc(side_out, 16)
            e.wait_ge(k_roped, 3)
            e.dma_start(kb_dram[:, META + CHUNK:KCOLS], ropx[:, 0:SEQ]).then_inc(side_out, 16)
            e.dma_start(kbcur[:, 0:META], ropx[:, SEQ:L]).then_inc(side_out, 16)
            e.wait_ge(side_out, 16 * 6)
            e.sem_inc(qb_free, 1)
            e.sem_inc(oT_free, 1)

            def pair_moves(hp, more):
                if more:
                    e.wait_ge(proj_summed, 7 * hp + 7)
                    e.dma_start(wpair[:, :, :], w_pair[bass.ds(hp + 1, 1)].rearrange("o p c n -> (o p) c n")
                                ).then_inc(wpair_in, 16)
                e.wait_ge(q_roped, 2 * hp + 2 + AHEAD)
                e.dma_start(qb_dram[:, bass.ds(hp, 1), :], ropx[:, 0:SEQ].rearrange("p (a n) -> p a n", a=1)
                            ).then_inc(qb_out, 16)
                e.wait_ge(qb_out, 16 * hp + 16)
                e.sem_inc(qb_free, 1)
                e.wait_ge(oT_ready, hp + 1 + 1)
                e.dma_start(oa_dram[:, bass.ds(hp, 1), :], oT.rearrange("p (a n) -> p a n", a=1)
                            ).then_inc(oa_out, 16)
                e.wait_ge(oa_out, 16 * hp + 16)
                e.sem_inc(oT_free, 1)

            with nc.sync.Fori(0, PAIRS - 1) as hp:
                pair_moves(hp, True)
            pair_moves(PAIRS - 1, False)

            def load_tile(t):
                cols = bass.ds(t * P, P)
                e.dma_start(qb[:, :, :], qb_dram[:, :, cols]).then_inc(tile_in, 16)
                e.dma_start(kbcur[:, META:WIN], kb_dram[:, bass.ds(t * P + META, 3 * CHUNK)]).then_inc(tile_in, 16)
                e.dma_start(vprev[META:PREV, :], vb_dram[bass.ds(t * P, CHUNK), :]).then_inc(tile_in, 16)
                e.dma_start(vown[:, :], vb_dram[bass.ds(t * P + CHUNK, P), :]).then_inc(tile_in, 16)
                e.dma_start(oa[:, :, :], oa_dram[:, :, cols]).then_inc(tile_in, 16)
                e.dma_start(hs[:, :], x[cols, :]).then_inc(tile_in, 16)

            e.wait_ge(oT_ready, PAIRS + 1)
            load_tile(0)
            e.dma_start(wout[:, :, :], w_out).then_inc(wout_in, 16)
            e.dma_start(wq[:, :, :], w_query).then_inc(wq_in, 16)
            e.sem_inc(h2_free, 1)

            def block_moves(b, more):
                if more:
                    e.wait_ge(h2_copied, b + 1)
                    load_tile(b + 1)
                e.wait_ge(out_ready, b + 1)
                e.dma_start(out[bass.ds(b * P, P), :], h2cur[:, :]).then_inc(out_done, 16)
                e.wait_ge(out_done, 16 * b + 16)
                e.sem_inc(h2_free, 1)

            with nc.sync.Fori(0, NT - 1) as b:
                block_moves(b, True)
            block_moves(NT - 1, False)
            e.wait_ge(out_done, 16 * NT)

        @block.gpsimd
        def _(pool):
            g = nc.gpsimd
            pool.sem_inc(xT_kept, AHEAD)
            g.memset(oT[:, 0:P], 0.0).then_inc(zeroed, 1)

            def keep_xT(n, u, rows):
                gate(pool, "pool", xT_ready, n + 1 + AHEAD)
                g.tensor_copy(xnT[:, :, bass.ds(n * P, rows)], xTc[:, u, :, 0:rows]).then_inc(xT_kept, 1)

            with g.Fori(0, NT // 2) as m:
                for u in range(2):
                    keep_xT(2 * m + u, u, P)
            keep_xT(NT, 0, META)

            with g.Fori(0, PAIRS) as hp:
                gate(pool, "pool", proj_summed, 7 * hp + 1)
                pool.wait_ge(v_kept, NT + 1 + AHEAD)
                g.tensor_copy(vpair[:, 0:NT, :], vall[:, 0:NT, bass.ds(hp * P, P)])
                g.tensor_copy(vpair[0:META, NT, :], vall[0:META, NT, bass.ds(hp * P, P)]
                              ).then_inc(vpair_ready, 1)
                for u, (j, t0, w, h) in enumerate(UNITS[:NADD]):
                    gate(pool, "pool", tri_done, NU * hp + u + 1)
                    own = P if t0 == P * j else 0
                    if own:
                        i = g.tensor_copy(acc[:, h, t0:t0 + P], sp[:, u % SPB, 0:P])
                    if w > own:
                        i = g.tensor_tensor(acc[:, h, t0 + own:t0 + w], acc[:, h, t0 + own:t0 + w],
                                            sp[:, u % SPB, own:w], ALU.add)
                    i.then_inc(acc_ready, 1)

            def gathers_of(b):
                for k in range(K):
                    if isinstance(b, int):
                        if k % TOPK == 0:
                            gate(pool, "pool", head_ready, k // TOPK + 1)
                    elif k % (K // 2) == 0:
                        gate(pool, "pool", idx_ready, 2 * b + k // (K // 2) + 1)
                    gate(pool, "pool", rows_used, K * b + k + 1)
                    g.indirect_dma_start(uv[:, k % NB, :], None, experts,
                                         bass.IndirectOffsetOnAxis(idxcur_u[:, k:k + 1], 0)
                                         ).then_inc(rows_in[k % NB], 16)

            gathers_of(0)
            with g.Fori(1, NT) as b:
                gathers_of(b)

        @block.scalar
        def _(act):
            a = nc.scalar
            own = Own(act, act_own)
            link = own.link
            act.sem_inc(v_kept, AHEAD)
            act.sem_inc(w_ready, ZB)
            act.sem_inc(gate_exp, 1)
            act.wait_ge(consts_in, 16)

            def log_exp_table():
                act.sem_inc(passed["act"], 1)
                a.preload_act_table_set("natural_log_exp_and_others")

            def rsqrt_mean(r, sums, n):
                log_exp_table()
                link(a.activation(r, sums, ACT.Ln, scale=1.0 / n, bias=epscol[0:r.shape[0], :]))
                return a.activation(r, r, ACT.Exp, scale=-0.5)

            act.wait_ge(eps_set, 1)

            def front(n, u, rows, m):
                act.wait_ge(x_in[u], 16 * m + 16)
                link(a.activation((hncur, h2cur)[u][0:rows, :], xt[0:rows, u, :], ACT.Square,
                                  accum_out=nssq[0:rows, u:u + 1]))
                rsqrt_mean(nr[0:rows, u:u + 1], nssq[0:rows, u:u + 1], D).then_inc(squared, 1)

            def back(n, u, rows):
                act.wait_ge(v_summed, n + 1 + AHEAD)
                a.activation(vall[0:rows, bass.ds(n, 1), 0:512], ps[0:rows, 4 + 2 * u:5 + 2 * u, :], ACT.Copy)
                a.activation(vall[0:rows, bass.ds(n, 1), 512:VW], ps[0:rows, 5 + 2 * u:6 + 2 * u, 0:P], ACT.Copy
                             ).then_inc(v_kept, 1)

            front(0, 0, P, 0)
            front(1, 1, P, 0)
            own.settle()
            with a.Fori(0, NT // 2 - 1) as m:
                for u in range(2):
                    front(2 * m + 2 + u, u, P, m + 1)
                    back(2 * m + u, u, P)
                own.settle()
            front(NT, 0, META, NT // 2)
            back(NT - 2, 0, P)
            back(NT - 1, 1, P)
            back(NT, 0, META)
            for i, (c0, w) in enumerate(SPANS):
                act.wait_ge(k_summed, i + 1)
                a.activation(ropx[:, c0:c0 + w], ps[:, i, 0:w], ACT.Copy).then_inc(k_kept, 1)

            kept = ([(qpair, c0, w, QSCALE) for c0, w in SPANS[:2]] + [(kpair, c0, w, 1.0) for c0, w in SPANS]
                    + [(ropx, c0, w, QSCALE) for c0, w in SPANS[:2]])
            own.settle()
            log_exp_table()
            with a.Fori(0, PAIRS) as hp:
                for i, (dst, c0, w, s) in enumerate(kept):
                    if i == 5:
                        gate(act, "act", qb_free, hp + 1)
                    act.wait_ge(proj_summed, 7 * hp + i + 1)
                    a.activation(dst[:, c0:c0 + w], ps[:, 4 + i % 2, 0:w], ACT.Copy, scale=s).then_inc(proj_kept, 1)

                def logs(u):
                    j, t0, w, h = UNITS[u]
                    r = P if j < NT else META
                    act.wait_ge(abs_ready, NU * hp + u + 1)
                    link(a.activation(az[0:r, u % 2, 0:w], az[0:r, u % 2, 0:w], ACT.Exp, scale=-1.0))
                    a.activation(az[0:r, u % 2, 0:w], az[0:r, u % 2, 0:w], ACT.Ln, bias=1.0).then_inc(log_ready, 1)

                def weights(u):
                    j, t0, w, h = UNITS[u]
                    r = P if j < NT else META
                    gate(act, "act", w_used, NU * hp + u + 1)
                    act.wait_ge(tri_done, NU * hp + u + 1)
                    a.activation(wb[0:r, u % 2, 0:w], ps[0:r, u % ZB, 0:w], ACT.Exp).then_inc(w_ready, 1)

                for u in range(NU + 2):
                    if u < NU:
                        logs(u)
                    if u >= 2:
                        weights(u - 2)
                own.settle()

            def tile_step(step, t):
                if step == "exp":
                    act.wait_ge(max_ready, t + 1)
                    for h in range(HEADS):
                        a.activation(ssb[:, h, :], ssb[:, h, :], ACT.Exp, bias=nmx[:, h:h + 1],
                                     accum_out=rs[:, h:h + 1])
                    a.activation(se, se, ACT.Exp).then_inc(exp_ready, 1)
                elif step == "pT":
                    for i in range(2):
                        act.wait_ge(pt_done, 4 * t + i + 1)
                        last = a.activation(pT[0:PREV, 0, 4 * i:4 * i + 4, :],
                                            grid(ps[0:PREV, 2 + i, :], 4), ACT.Copy)
                    last.then_inc(pt_kept_a, 1)
                elif step == "ob":
                    act.wait_ge(tile_in, 96 * t + 96)
                    a.activation(sq[:, 0:4, :], oa[:, :, :], ACT.Square)
                    act.wait_ge(ob_done, t + 1)
                    a.activation(sq[:, 4:8, :], grid(ps[:, 6, :], 4), ACT.Square)
                    a.activation(ob[:, :, :], grid(ps[:, 6, :], 4), ACT.Copy).then_inc(ob_ready, 1)
                elif step == "h2sq":
                    act.wait_ge(h2_ready, t + 1)
                    link(a.activation(hnn[:, :], hs[:, :], ACT.Square, accum_out=r3[:, 0:1]))
                    rsqrt_mean(r3[:, 1:2], r3[:, 0:1], D).then_inc(h2_squared, 1)
                elif step == "r2":
                    act.wait_ge(ssq_done, t + 1)
                    rsqrt_mean(r2, ps[:, 7, 0:2], HEADS * HD).then_inc(r2_ready, 1)
                elif step == "hnT":
                    for i in range(2):
                        act.wait_ge(hnT_done, 2 * t + i + 1)
                        a.activation(hnT[:, 4 * i:4 * i + 4, :], grid(ps[:, 2 + i, :], 4), ACT.Copy
                                     ).then_inc(hnT_kept, 1)
                elif step == "qT":
                    for i in range(2):
                        act.wait_ge(qT_done, PH * t + 4 * i + 4)
                        a.activation(qT[:, 4 * i:4 * i + 4, :], grid(ps[:, 4 + i, :], 4), ACT.Copy
                                     ).then_inc(qT_kept, 1)
                elif step == "keys":
                    for i, bank in enumerate(KEY_BANKS):
                        act.wait_ge(key_done, 4 * t + i + 1)
                        a.activation(s_all[:, 4 * i:4 * i + 4, :], grid(ps[:, bank, :], 4), ACT.Copy
                                     ).then_inc(key_kept, 1)
                elif step == "gexp":
                    act.wait_ge(gate_in, t + 1)
                    a.activation(gn, gn, ACT.Exp).then_inc(gate_exp, 1)

            def head_gates(h):
                act.wait_ge(head_in, h + 1)
                a.activation(gn3[:, h, :], gn3[:, h, :], ACT.Exp).then_inc(head_exp, 1)

            at = {8: "exp", 11: "pT", 14: "ob", 16: "r2", 21: "h2sq", 24: "hnT", 33: "qT", 35: "keys", 55: "gexp"}
            for step in at.values():
                if step == "gexp":
                    head_gates(0)
                else:
                    tile_step(step, 0)
                if step == "ob":
                    act.wait_ge(wout_in, 16)
                    for c in range(2 * PAIRS):
                        last = a.activation(wout[:, c, :], wout[:, c, :], ACT.Copy, scale=mixgain[:, c:c + 1])
                    last.then_inc(wout_scaled, 1)

            def experts_of(b, more):
                for n in range(NG):
                    act.wait_ge(dotted, K * b + GRP * (n + 1))
                    a.activation(gel[:, GRP * n:GRP * n + GRP], actv[:, GRP * n:GRP * n + GRP], ACT.Gelu
                                 ).then_inc(gelu_ready, 1)
                    if isinstance(b, int) and b == 0 and 1 <= n < PH:
                        head_gates(n)
                    if more and n in at:
                        tile_step(at[n], b + 1)
                act.wait_ge(h3_ready, b + 1 + 1)
                link(a.activation(hncur[:, :], h2cur[:, :], ACT.Square, accum_out=r4[:, 0:1]))
                rsqrt_mean(r4[:, 1:2], r4[:, 0:1], D).then_inc(h3_squared, 1)

            own.settle()
            experts_of(0, True)
            own.settle()
            with a.Fori(1, NT - 1) as b:
                experts_of(b, True)
                own.settle()
            experts_of(NT - 1, False)

        @block.vector
        def _(dve):
            v = nc.vector
            own = Own(dve, dve_own)
            link = own.link
            dve.sem_inc(xT_ready, AHEAD)
            dve.sem_inc(q_roped, AHEAD)
            dve.sem_inc(oT_ready, 1)
            dve.sem_inc(routed, 2)
            dve.sem_inc(idx_ready, 2)
            dve.sem_inc(gate_in, 1)
            dve.sem_inc(h3_ready, 1)
            v.memset(onecol, 1.0)
            v.memset(epscol, EPS).then_inc(eps_set, 1)
            dve.wait_ge(consts_in, 16)

            def polish(r, sums, n):
                rows, w = r.shape
                m, q = (newton[0:rows, w * i:w * i + w] for i in range(2))
                v.tensor_scalar(m, sums, 1.0 / n, EPS, ALU.mult, ALU.add)
                link(v.tensor_tensor(q, r, r, ALU.mult))
                link(v.tensor_tensor(q, q, m, ALU.mult))
                link(v.tensor_scalar(q, q, -0.5, 1.5, ALU.mult, ALU.add))
                link(v.tensor_tensor(r, r, q, ALU.mult))

            def front(n, u, rows):
                dve.wait_ge(squared, n + 1)
                polish(nr[0:rows, u:u + 1], nssq[0:rows, u:u + 1], D)
                v.tensor_scalar(xt[0:rows, u, :], xt[0:rows, u, :], nr[0:rows, u:u + 1], None, ALU.mult
                                ).then_inc(scaled, 1)

            def back(n, u, rows):
                dve.wait_ge(xT_kept, n + 1)
                dve.wait_ge(v_summed, n + 1)
                dve.wait_ge(turned, n + 1)
                for c in range(0, DC, 4):
                    last = v.tensor_tensor(
                        xTc[:, u, c:c + 4, 0:rows], grid(ps[:, 2 * u + c // 4, :], 4)[:, :, 0:rows],
                        lnmix[:, c:c + 4].unsqueeze(2).to_broadcast([P, 4, rows]), ALU.mult)
                last.then_inc(xT_ready, 1)

            front(0, 0, P)
            own.settle()
            with v.Fori(0, NT // 2 - 1) as m:
                front(2 * m + 1, 1, P)
                back(2 * m, 0, P)
                front(2 * m + 2, 0, P)
                back(2 * m + 1, 1, P)
                own.settle()
            front(NT - 1, 1, P)
            back(NT - 2, 0, P)
            front(NT, 0, META)
            back(NT - 1, 1, P)
            back(NT, 0, META)

            def rotate(bank, c0, w):
                cols = slice(c0, c0 + w)
                v.tensor_tensor(ropt[:, cols], ps[:, bank, 0:w], sin[:, cols], ALU.mult)
                link(v.tensor_tensor(ropx[:, cols], ropx[:, cols], cos[:, cols], ALU.mult))
                return v.tensor_tensor(ropx[:, cols], ropx[:, cols], ropt[:, cols], ALU.add)

            for i, (c0, w) in enumerate(SPANS):
                dve.wait_ge(k_turned, i + 1)
                rotate(3 + i, c0, w).then_inc(k_roped, 1)

            own.settle()
            with v.Fori(0, PAIRS) as hp:
                for i, (c0, w) in enumerate(SPANS[:2]):
                    dve.wait_ge(q_turned, 2 * hp + i + 1)
                    rotate(4 + i, c0, w).then_inc(q_roped, 1)

                def magnitude(u):
                    j, t0, w, h = UNITS[u]
                    r = P if j < NT else META
                    if u >= 2:
                        dve.wait_ge(sp_ready, NU * hp + u - 1)
                    dve.wait_ge(z_ready, NU * hp + u + 1)
                    v.tensor_scalar(az[0:r, u % 2, 0:w].bitcast(U32), ps[0:r, u % ZB, 0:w].bitcast(U32),
                                    0x7FFFFFFF, None, ALU.bitwise_and).then_inc(abs_ready, 1)

                def softplus(u):
                    j, t0, w, h = UNITS[u]
                    r = P if j < NT else META
                    if u >= SPB:
                        dve.wait_ge(acc_ready, NADD * hp + min(u - SPB + 1, NADD))
                    dve.wait_ge(log_ready, NU * hp + u + 1)
                    i = v.scalar_tensor_tensor(out=sp[0:r, u % SPB, 0:w], in0=ps[0:r, u % ZB, 0:w], scalar=0.0,
                                               in1=az[0:r, u % 2, 0:w], op0=ALU.max, op1=ALU.add)
                    if t0 == P * j:
                        link(i)
                        i = v.tensor_tensor(sp[:, u % SPB, 0:P], sp[:, u % SPB, 0:P], mask01, ALU.mult)
                    i.then_inc(sp_ready, 1)

                for u in range(NU + 1):
                    if u < NU:
                        magnitude(u)
                    if u >= 1:
                        softplus(u - 1)
                dve.wait_ge(oT_free, hp + 1)
                dve.wait_ge(w_used, NU * hp + NU + AHEAD)
                v.tensor_copy(grid(oT, 2), ps[:, 6:8, :]).then_inc(oT_ready, 1)
                own.settle()

            def top16(values, places, scores, rest, rows):
                for row in rows:
                    last = v.max(values[:, row, 0:8], scores[:, row, :])
                link(last)
                for row in rows:
                    v.max_index(places[:, row, 0:8], values[:, row, 0:8], scores[:, row, :])
                    last = v.match_replace(rest[:, row, :], values[:, row, 0:8], scores[:, row, :], -3e38)
                link(last)
                for row in rows:
                    last = v.max(values[:, row, 8:16], rest[:, row, :])
                link(last)
                for row in rows:
                    last = v.max_index(places[:, row, 8:16], values[:, row, 8:16], rest[:, row, :])
                link(last)

            dve.wait_ge(side_in, 16 * N_SIDE)

            def tile_step(step, t):
                if step == "mask":
                    dve.wait_ge(score_done, t + 1)
                    m = winmask[:, 0 if isinstance(t, int) and t == 0 else 1, :]
                    for i in range(4):
                        last = v.tensor_tensor(ssb[:, 2 * i:2 * i + 2, :], grid(ps[:, 2 + i, 0:2 * WIN], 2),
                                               m.unsqueeze(1).to_broadcast([P, 2, WIN]), ALU.add)
                    link(last)
                    link(v.tensor_reduce(mx, ssb[:, :, :], AX.X, ALU.max))
                    link(v.tensor_tensor(mx, mx, sinkb[:, :], ALU.max))
                    v.tensor_tensor(se, sinkb[:, :], mx, ALU.subtract)
                    v.tensor_scalar(nmx, mx, -1.0, None, ALU.mult).then_inc(max_ready, 1)
                elif step == "norm":
                    dve.wait_ge(exp_ready, t + 1)
                    link(v.tensor_tensor(rden, rs, se, ALU.add))
                    link(v.reciprocal(rden, rden))
                    v.tensor_tensor(ssb[:, :, :], ssb[:, :, :], rden.unsqueeze(2).to_broadcast([P, HEADS, WIN]),
                                    ALU.mult).then_inc(p_ready, 1)
                elif step == "pT":
                    for i in range(2):
                        dve.wait_ge(pt_done, 4 * t + i + 3)
                        last = v.tensor_copy(pT[:, 1, 4 * i:4 * i + 4, :], grid(ps[:, 4 + i, :], 4))
                    last.then_inc(pt_kept_v, 1)
                elif step == "r2":
                    dve.wait_ge(r2_ready, t + 1)
                    polish(r2, ps[:, 7, 0:2], HEADS * HD)
                elif step == "h2":
                    dve.wait_ge(mix_done, 4 * t + 4)
                    hg = grid(hs, 2)
                    link(v.scalar_tensor_tensor(out=hg, in0=ps[:, 2:4, :], scalar=r2[:, 0:1], in1=hg,
                                                op0=ALU.mult, op1=ALU.add))
                    v.scalar_tensor_tensor(out=hg, in0=ps[:, 4:6, :], scalar=r2[:, 1:2], in1=hg,
                                           op0=ALU.mult, op1=ALU.add).then_inc(h2_ready, 1)
                elif step == "hn":
                    dve.wait_ge(h2_squared, t + 1)
                    polish(r3[:, 1:2], r3[:, 0:1], D)
                    v.scalar_tensor_tensor(out=hnn, in0=hs, scalar=r3[:, 1:2], in1=lnb[:, :],
                                           op0=ALU.mult, op1=ALU.mult).then_inc(hn_ready, 1)
                elif step == "cands":
                    link(v.tensor_copy(topf[:, :, :], topi[:, :, :]))
                    link(v.tensor_scalar(topf[:, 0:PH, :], topf[:, 0:PH, :], float(NKEYS), None, ALU.mult))
                    for both, into in ((topv, cs), (topf, ci)):
                        for a0, na, nb, at in SEGS:
                            last = v.tensor_tensor(
                                into[:, :, at:at + na * nb].rearrange("p h (a b) -> p h a b", a=na),
                                both[:, 0:PH, a0:a0 + na].unsqueeze(3).to_broadcast([P, PH, na, nb]),
                                both[:, PH:2 * PH, 0:nb].unsqueeze(2).to_broadcast([P, PH, na, nb]), ALU.add)
                    link(last)
                elif step == "gate":
                    v.tensor_tensor(gn3, tops[:, :, :], tops[:, :, 0:1].to_broadcast([P, PH, TOPK]),
                                    ALU.subtract).then_inc(gate_in, 1)
                    link(v.tensor_copy(idxn_u, idxf))
                elif step == "routed":
                    dve.wait_ge(gate_exp, t + 1)
                    link(v.tensor_reduce(gsum, gn3, AX.X, ALU.add))
                    link(v.reciprocal(gsum, gsum))
                    v.tensor_tensor(gn3, gn3, gsum.unsqueeze(2).to_broadcast([P, PH, TOPK]), ALU.mult
                                    ).then_inc(routed, 1)
                    v.tensor_copy(idxcur_u[:, 0:K // 2], idxn_u[:, 0:K // 2]).then_inc(idx_ready, 1)
                elif step[0] == "top":
                    if step[1] == 0:
                        gate(dve, "dve", key_kept, 4 * t + 4)
                    top16(topv, topi, s_all, s_tmp, (2 * step[1], 2 * step[1] + 1))
                elif step[0] == "pick":
                    h = step[1]
                    top16(tops, pos, cs, cs2, (h,))
                    link(v.tensor_copy(posf[:, h, :], pos[:, h, :]))
                    for k in range(TOPK):
                        last = v.scalar_tensor_tensor(out=eq[:, k, :], in0=iota, scalar=posf[:, h, k:k + 1],
                                                      in1=ci[:, h, :], op0=ALU.is_equal, op1=ALU.mult,
                                                      accum_out=idxf3[:, h, k:k + 1])
                    link(last)

            at = {7: "mask", 9: "norm", 12: "pT", 17: "r2", 20: "h2", 22: "hn", 45: "cands", 54: "gate",
                  57: "routed"}
            at.update({37 + i: ("top", i) for i in range(PH)})
            at.update({46 + i: ("pick", i) for i in range(PH)})

            def head_experts(h):
                tile_step(("pick", h), 0)
                v.tensor_copy(idxcur_u[:, TOPK * h:TOPK * h + TOPK], idxf3[:, h, :]).then_inc(head_ready, 1)
                v.tensor_tensor(gn3[:, h, :], tops[:, h, :], tops[:, h, 0:1].to_broadcast([P, TOPK]),
                                ALU.subtract).then_inc(head_in, 1)

            def head_gates(h):
                dve.wait_ge(head_exp, h + 1)
                link(v.tensor_reduce(gsum[:, h:h + 1], gn3[:, h, :], AX.X, ALU.add))
                link(v.reciprocal(gsum[:, h:h + 1], gsum[:, h:h + 1]))
                link(v.tensor_scalar(gcur3[:, h, :], gn3[:, h, :], gsum[:, h:h + 1], None, ALU.mult))

            for n in sorted(at):
                if n < 46:
                    tile_step(at[n], 0)
            head_experts(0)
            link(v.tensor_copy(hncur[:, :], hnn))
            head_gates(0)

            def experts_of(b, more):
                first = isinstance(b, int) and b == 0
                if not first:
                    v.tensor_copy(idxcur_u[:, K // 2:K], idxn_u[:, K // 2:K]).then_inc(idx_ready, 1)
                    v.tensor_copy(hncur[:, :], hnn)
                    dve.wait_ge(routed, b + 1 + 1)
                    link(v.tensor_copy(gcur, gn))
                for n in range(NG + 1):
                    if n < NG:
                        for k in range(GRP * n, GRP * n + GRP):
                            dve.wait_ge(rows_in[k % NB], (16 * K // NB) * b + 16 * (k // NB + 1))
                            v.tensor_tensor_reduce(uv[:, k % NB, 0:D], uv[:, k % NB, 0:D], hncur[:, :], 1.0, 0.0,
                                                   ALU.mult, ALU.add, actv[:, k:k + 1]).then_inc(dotted, 1)
                    if n == 2:
                        dve.wait_ge(h2_free, b + 1)
                        v.tensor_copy(h2cur[:, :], hs).then_inc(h2_copied, 1)
                    if n > 0:
                        m = n - 1
                        dve.wait_ge(rows_used, K * b + GRP * m + GRP - 4 + NB)
                        dve.wait_ge(gelu_ready, NG * b + m + 1)
                        for k in range(GRP * m, GRP * m + GRP):
                            v.tensor_scalar(diag[:, k % 4, :], ident, gel[:, k:k + 1], gcur[:, k:k + 1],
                                            ALU.mult, ALU.mult).then_inc(diag_ready, 1)
                    if first and n + 1 < PH:
                        head_experts(n + 1)
                    if first and 2 <= n <= PH:
                        head_gates(n - 1)
                    if more and n in at:
                        tile_step(at[n], b + 1)
                dve.wait_ge(rows_used, K * b + K + NB)
                hg = h2cur[:, :].rearrange("p (a n) -> p a n", a=2)
                v.tensor_tensor(hg, ps[:, 0:2, :], hg, ALU.add).then_inc(h3_ready, 1)
                dve.wait_ge(h3_squared, b + 1)
                polish(r4[:, 1:2], r4[:, 0:1], D)
                v.scalar_tensor_tensor(out=h2cur[:, :], in0=h2cur[:, :], scalar=r4[:, 1:2], in1=fnb[:, :],
                                       op0=ALU.mult, op1=ALU.mult).then_inc(out_ready, 1)

            own.settle()
            experts_of(0, True)
            own.settle()
            with v.Fori(1, NT - 1) as b:
                experts_of(b, True)
                own.settle()
            experts_of(NT - 1, False)

        @block.tensor
        def _(pe):
            t_ = nc.tensor
            pe.sem_inc(v_summed, AHEAD)
            pe.sem_inc(w_used, AHEAD)
            pe.sem_inc(rows_used, NB)
            pe.wait_ge(consts_in, 16)

            def front(n, u, rows):
                pe.wait_ge(xT_ready, n + 1)
                pe.wait_ge(scaled, n + 1)
                for c in range(DC):
                    last = t_.transpose(ps[:, 2 * u + c // 4, P * (c % 4):P * (c % 4) + rows],
                                        xt[0:rows, u, P * c:P * c + P], ident[0:rows, 0:rows])
                last.then_inc(turned, 1)

            def back(n, u, rows):
                pe.wait_ge(v_kept, n + 1)
                pe.wait_ge(xT_ready, n + 1 + AHEAD)
                for bank, c0, w in ((4 + 2 * u, 0, 512), (5 + 2 * u, 512, P)):
                    for c in range(DC):
                        last = t_.matmul(ps[0:rows, bank, 0:w], xTc[:, u, c, 0:rows], wv[:, c, c0:c0 + w],
                                         start=c == 0, stop=c == DC - 1)
                last.then_inc(v_summed, 1)

            front(0, 0, P)
            pe.wait_ge(wv_in, 16)
            with t_.Fori(0, NT // 2 - 1) as m:
                front(2 * m + 1, 1, P)
                back(2 * m, 0, P)
                front(2 * m + 2, 0, P)
                back(2 * m + 1, 1, P)
            front(NT - 1, 1, P)
            back(NT - 2, 0, P)
            front(NT, 0, META)
            back(NT - 1, 1, P)
            back(NT, 0, META)

            pe.wait_ge(wkb_in, 32)
            pe.wait_ge(xT_kept, NT + 1 + AHEAD)
            for i, (c0, w) in enumerate(SPANS):
                for c in range(DC):
                    last = t_.matmul(ps[:, i, 0:w], wkb[:, c, :], xnT[:, c, c0:c0 + w], start=c == 0,
                                     stop=c == DC - 1)
                last.then_inc(k_summed, 1)
            pe.wait_ge(v_kept, NT + 1 + AHEAD)
            for i, (c0, w) in enumerate(SPANS):
                pe.wait_ge(k_kept, i + 1)
                t_.matmul(ps[:, 3 + i, 0:w], perm, ropx[:, c0:c0 + w], start=True, stop=True).then_inc(k_turned, 1)
            pe.wait_ge(k_roped, len(SPANS))

            proj = ([(0, c0, w) for c0, w in SPANS[:2]] + [(P, c0, w) for c0, w in SPANS]
                    + [(2 * P, c0, w) for c0, w in SPANS[:2]])
            with t_.Fori(0, PAIRS) as hp:
                for i, (col, c0, w) in enumerate(proj):
                    if i == 0:
                        pe.wait_ge(wpair_in, 16 * hp + 16)
                        pe.wait_ge(q_roped, 2 * hp + AHEAD)
                    if i >= 2:
                        pe.wait_ge(proj_kept, 7 * hp + i - 1)
                    for c in range(DC):
                        last = t_.matmul(ps[:, 4 + i % 2, 0:w], wpair[:, c, col:col + P], xnT[:, c, c0:c0 + w],
                                         start=c == 0, stop=c == DC - 1)
                    last.then_inc(proj_summed, 1)
                pe.wait_ge(proj_kept, 7 * hp + 7)
                for i, (c0, w) in enumerate(SPANS[:2]):
                    t_.matmul(ps[:, 4 + i, 0:w], perm, ropx[:, c0:c0 + w], start=True, stop=True
                              ).then_inc(q_turned, 1)

                def scores(u):
                    j, t0, w, h = UNITS[u]
                    r = P if j < NT else META
                    rows = slice(HD * h, HD * h + HD)
                    gate(pe, "pe", w_ready, NU * hp + u + 1)
                    t_.matmul(ps[0:r, u % ZB, 0:w], kpair[rows, P * j:P * j + r], qpair[rows, t0:t0 + w],
                              start=True, stop=False, skip_group_check=True).then_inc(z_ready, 1)

                def later(u):
                    j, t0, w, h = UNITS[u]
                    r = P if j < NT else META
                    own = P if t0 == P * j else 0
                    last_add = max([p for p in range(min(u, NADD)) if UNITS[p][3] == h
                                    and UNITS[p][1] < t0 + w and t0 < UNITS[p][1] + UNITS[p][2]] + [-1])
                    gate(pe, "pe", sp_ready, NU * hp + u + 1)
                    if w > own:
                        gate(pe, "pe", acc_ready, NADD * hp + last_add + 1)
                    last = t_.matmul(ps[0:r, u % ZB, 0:w], negtri[0:r, 0:r], sp[0:r, u % SPB, 0:w], start=False,
                                     stop=not own and w == own, skip_group_check=True)
                    if own:
                        last = t_.matmul(ps[:, u % ZB, 0:P], ident, maskneg, start=False, stop=w == own,
                                         skip_group_check=True)
                    if w > own:
                        last = t_.matmul(ps[0:r, u % ZB, own:w], negones[:, 0:r], acc[:, h, t0 + own:t0 + w],
                                         start=False, stop=True, skip_group_check=True)
                    last.then_inc(tri_done, 1)

                def weigh(u):
                    j, t0, w, h = UNITS[u]
                    r = P if j < NT else META
                    first = not any(x[3] == h and x[1] // 512 == t0 // 512 for x in UNITS[:u])
                    gate(pe, "pe", w_ready, NU * hp + u + 1 + ZB)
                    t_.matmul(ps[HD * h:HD * h + HD, 6 + t0 // 512, t0 % 512:t0 % 512 + w],
                              vpair[0:r, j, HD * h:HD * h + HD], wb[0:r, u % 2, 0:w], start=first,
                              stop=j == NT, skip_group_check=True).then_inc(w_used, 1)

                for u in range(NU + 3):
                    if u < NU:
                        scores(u)
                    if 2 <= u < NU + 2:
                        later(u - 2)
                    if u == 3:
                        pe.wait_ge(vpair_ready, hp + 1)
                        pe.wait_ge(oT_ready, hp + 1)
                    if u >= 3:
                        weigh(u - 3)
            pe.wait_ge(oT_ready, PAIRS + 1)

            pe.wait_ge(side_in, 16 * N_SIDE)

            def tile_step(step, t):
                if step == "scores":
                    pe.wait_ge(routed, t + 1)
                    pe.wait_ge(tile_in, 96 * t + 96)
                    for c in range(4):
                        for h in range(2):
                            rows = slice(HD * h, HD * h + HD)
                            last = t_.matmul(ps[:, 2 + 2 * h + c // 2, WIN * (c % 2):WIN * (c % 2) + WIN],
                                             qb[rows, c, :], kbcur[rows, :], start=True, stop=True)
                    last.then_inc(score_done, 1)
                elif step == "pT":
                    pe.wait_ge(p_ready, t + 1)
                    for own, w in ((0, PREV), (1, P)):
                        for i in range(2):
                            for h in range(4):
                                last = t_.transpose(ps[0:w, 2 + 2 * own + i, P * h:P * h + P],
                                                    ssb[:, 4 * i + h, PREV * own:PREV * own + w], ident)
                            last.then_inc(pt_done, 1)
                elif step == "pv":
                    pe.wait_ge(pt_kept_a, t + 1)
                    pe.wait_ge(pt_kept_v, t + 1)
                    for h in range(2):
                        cols = slice(HD * h, HD * h + HD)
                        t_.matmul(ps[cols, 6, :], vprev[0:PREV, cols], pT[0:PREV, 0, 4 * h:4 * h + 4, :],
                                  start=True, stop=False)
                        last = t_.matmul(ps[cols, 6, :], vown[:, cols], pT[:, 1, 4 * h:4 * h + 4, :],
                                         start=False, stop=True)
                    last.then_inc(ob_done, 1)
                elif step == "ssq":
                    pe.wait_ge(ob_ready, t + 1)
                    for i in range(8):
                        last = t_.matmul(ps[:, 7, i // 4:i // 4 + 1], sq[:, i, :], onecol, start=i % 4 == 0,
                                         stop=i % 4 == 3)
                    last.then_inc(ssq_done, 1)
                elif step[0] == "mix":
                    i = step[1]
                    pe.wait_ge(wout_scaled, 1)
                    for c in range(4):
                        last = t_.matmul(ps[:, 2 + i, :], (oa, ob)[i // 2][:, c, :],
                                         wout[:, 4 * (i // 2) + c, 512 * (i % 2):512 * (i % 2) + 512],
                                         start=c == 0, stop=c == 3)
                    last.then_inc(mix_done, 1)
                elif step == "hnT":
                    pe.wait_ge(hn_ready, t + 1)
                    for c in range(DC):
                        last = t_.transpose(ps[:, 2 + c // 4, P * (c % 4):P * (c % 4) + P], hnn[:, P * c:P * c + P],
                                            ident)
                        if c % 4 == 3:
                            last.then_inc(hnT_done, 1)
                elif step[0] == "query":
                    h = step[1]
                    if h == 0:
                        pe.wait_ge(wq_in, 16)
                        pe.wait_ge(hnT_kept, 2 * t + 2)
                    for c in range(DC):
                        last = t_.matmul(ps[:, 4 + h // 4, P * (h % 4):P * (h % 4) + P], wq[:, c, P * h:P * h + P],
                                         hnT[:, c, :], start=c == 0, stop=c == DC - 1)
                    last.then_inc(qT_done, 1)
                elif step == "keys":
                    pe.wait_ge(qT_kept, 2 * t + 2)
                    for i, bank in enumerate(KEY_BANKS):
                        rows = slice(HD * (i // 2), HD * (i // 2) + HD)
                        for h in range(4):
                            last = t_.matmul(ps[:, bank, P * h:P * h + P], qT[rows, 4 * (i % 2) + h, :],
                                             keysT[rows, 4 * (i % 2) + h, :], start=True, stop=True)
                        last.then_inc(key_done, 1)

            at = {5: "scores", 10: "pT", 13: "pv", 14: "ssq", 23: "hnT", 34: "keys"}
            at.update({15 + i: ("mix", i) for i in range(4)})
            at.update({25 + i: ("query", i) for i in range(PH)})
            for n in sorted(at):
                tile_step(at[n], 0)

            def experts_of(b, more):
                for n in range(NG):
                    for k in range(GRP * n, GRP * n + GRP):
                        if k == 0:
                            pe.wait_ge(h3_ready, b + 1)
                        pe.wait_ge(diag_ready, K * b + k + 1)
                        for i in range(2):
                            last = t_.matmul(ps[:, i, :], diag[:, k % 4, :],
                                             uv[:, k % NB, D + 512 * i:D + 512 * i + 512], start=k == 0,
                                             stop=k == K - 1)
                        last.then_inc(rows_used, 1)
                    if more and n in at:
                        tile_step(at[n], b + 1)

            with t_.Fori(0, NT - 1) as b:
                experts_of(b, True)
            experts_of(NT - 1, False)


def constants():
    f = np.float32
    s, t = np.arange(P)[:, None], np.arange(P)[None, :]
    c = np.zeros((P, C_ALL), f)
    c[:, C_ID:C_ID + P] = s == t
    c[:, C_TRI:C_TRI + P] = -(s >= t).astype(f)
    c[:, C_ONES:C_ONES + P] = -1
    c[:, C_M01:C_M01 + P] = s < t
    c[:, C_MNEG:C_MNEG + P] = np.where(s < t, 0, NEG)
    c[:, C_PERM:C_PERM + P] = s == (t // HD) * HD + (t + HD // 2) % HD
    c[:, C_IOTA:C_IOTA + NC] = np.arange(NC)
    part = np.concatenate([[0] * META, [1] * CHUNK, [2] * CHUNK, [3] * CHUNK])[None, :]
    chunk = s // CHUNK
    seen = (part == 0) | (part == 1 + chunk) | (part == 2 + chunk)
    c[:, C_WM:C_WM + WIN] = np.where(seen & (part != 1), 0, NEG)
    c[:, C_WM + WIN:C_WM + 2 * WIN] = np.where(seen, 0, NEG)
    return c


def rope_table():
    f = np.float32
    half = HD // 2
    freq = f(10000.0) ** (-np.arange(half, dtype=f) / f(half))
    position = np.concatenate([np.arange(META, L), np.arange(META)]).astype(f)
    angle = (position[None, :] * np.tile(freq, P // half)[:, None]).astype(f)
    sign = np.where(np.arange(P) % HD < half, f(-1), f(1))[:, None]
    return np.concatenate([np.cos(angle), sign * np.sin(angle)], axis=1).astype(f)


def kernel(x, meta_tokens, ln_mix, w_in, sb_out_norm, swa_out_norm, sinks, w_out, ln_ffn, peer_query,
           peer_sub_keys, expert_u, expert_v, final_norm):
    from concourse import bacc
    from concourse.bass_utils import run_bass_kernel_spmd

    def rows(w):
        return w.reshape(-1, P, w.shape[-1]).transpose(1, 0, 2)

    w_in, w_out = np.asarray(w_in)[0], np.asarray(w_out)[0]
    width = HEADS * HD
    order = np.arange(width).reshape(2, PAIRS, HD).transpose(1, 0, 2).reshape(-1)
    qa, ka, va, qb, kb, vb = np.split(w_in, [width, 2 * width, 3 * width, 4 * width, 4 * width + P], axis=1)
    qb = qb[:, order]
    w_pair = np.stack([rows(np.concatenate([m[:, P * i:P * i + P] for m in (qa, ka, qb)], axis=1))
                       for i in range(PAIRS)])
    w_out = np.concatenate([w_out[:width], w_out[width:][order]])
    gains = np.concatenate([np.asarray(sb_out_norm)[0], np.asarray(swa_out_norm)[0][order]])
    consts = constants()
    consts[:, C_GAIN:C_GAIN + 8] = gains.reshape(8, P).T
    consts[:, C_LNM:C_LNM + DC] = np.asarray(ln_mix)[0].reshape(DC, P).T
    keys_t = np.asarray(peer_sub_keys)[0].transpose(1, 3, 0, 2).reshape(P, PH, NKEYS)
    given = [
        ("x", np.asarray(x)[0]), ("meta", np.asarray(meta_tokens)), ("w_pair", w_pair),
        ("w_v", rows(np.concatenate([va, vb], axis=1))), ("w_kb", rows(kb)), ("consts", consts),
        ("rope_cs", rope_table()), ("w_out", rows(w_out)), ("sinks", np.asarray(sinks)[0]),
        ("ln_ffn", np.asarray(ln_ffn)[0]), ("fnorm", np.asarray(final_norm)),
        ("w_query", rows(np.asarray(peer_query)[0])), ("keys_t", keys_t),
        ("experts", np.concatenate([np.asarray(expert_u)[0], np.asarray(expert_v)[0]], axis=1)),
    ]
    nc = bacc.Bacc("TRN2", target_bir_lowering=False, num_devices=1)
    arrays, args = {}, []
    for name, array in given:
        arrays["in_" + name] = np.ascontiguousarray(array)
        args.append(nc.dram_tensor("in_" + name, array.shape, F32, kind="ExternalInput").ap())
    out = nc.dram_tensor("result", (SEQ, D), F32, kind="ExternalOutput").ap()
    block_program(nc, *args, out)
    got = run_bass_kernel_spmd(nc, [arrays], core_ids=[0]).results[0]["result"]
    return got.reshape(1, SEQ, D)
```

```python
from contextlib import ExitStack

import numpy as np

import concourse.bass as bass
from concourse import mybir

F32 = mybir.dt.float32
U32 = mybir.dt.uint32
ALU = mybir.AluOpType
ACT = mybir.ActivationFunctionType
AX = mybir.AxisListType

P = 128
D = 1024
SEQ = 1024
META = 16
HD = 64
HEADS = 8
PAIRS = HEADS // 2
DC = D // P
NT = SEQ // P
L = SEQ + META
QKW = 3 * P
VW = HEADS * HD + P
CHUNK = 64
WIN = META + 3 * CHUNK
PREV = META + CHUNK
KCOLS = META + CHUNK + SEQ
EPS = 1e-6
QSCALE = HD ** -0.5
NKEYS = 128
NEXP = NKEYS * NKEYS
TOPK = 16
PH = 8
K = PH * TOPK
NEG = -1e30
NB = 8
GRP = 2
NG = K // GRP
SEGS = []
_at = 0
for _a0, _na in ((0, 1), (1, 1), (2, 1), (3, 1), (4, 1), (5, 3), (8, 8)):
    _nb = TOPK // (_a0 + 1)
    SEGS.append((_a0, _na, _nb, _at))
    _at += _na * _nb
NC = _at

def units_of(first, end):
    units = []
    for j in list(range(NT - 1, -1, -1)) + [NT]:
        t = max(P * j if j < NT else 0, first)
        while t < end:
            w = min(512 - t % 512, end - t)
            units += [(j, t, w, 0), (j, t, w, 1)]
            t += w
    return units


LAST = PAIRS - 1
EARLY, LATE = units_of(0, 512), units_of(512, SEQ)
LAST_TO = 512 + P
LAST_EARLY, LAST_LATE = units_of(0, LAST_TO), units_of(LAST_TO, SEQ)
assert PAIRS * P == 512 and [u[::3] for u in LATE] == [u[::3] for u in LAST_LATE]


def late_list(b):
    return LAST_LATE if isinstance(b, int) and b == LAST else LATE


SPANS = ((0, 512), (512, 512), (SEQ, META))
KEY_BANKS = (2, 3, 6, 7)
AHEAD = 2
ZB = 4
SPB = 4
assert len(EARLY) % 2 == 0
LATE_AT = [34 + 5 * _u // 4 for _u in range(len(LATE))]
NL = len(LATE)
HEAD_AT = (0, 2, 4, 5, 7, 9, 10)
LKB = 6
NLADD = sum(u[0] < NT for u in LATE)


def adds(units):
    return sum(u[0] < NT for u in units)


def late_units(group):
    return [u for u, at in enumerate(LATE_AT) if at == group]


C_ID, C_TRI, C_ONES, C_M01, C_MNEG, C_PERM = (P * i for i in range(6))
C_IOTA = 6 * P
C_WM = C_IOTA + NC
C_GAIN = C_WM + 2 * WIN
C_LNM = C_GAIN + 8
C_ALL = C_LNM + DC


class Own:

    def __init__(self, engine, semaphore):
        self.engine, self.semaphore, self.n = engine, semaphore, 0

    def link(self, instruction):
        self.n += 1
        instruction.then_inc(self.semaphore, 1)
        self.engine.wait_ge(self.semaphore, self.n)

    def settle(self):
        if self.n:
            self.engine.wait_ge(self.semaphore, self.n)
            self.engine.sem_clear(self.semaphore)
            self.n = 0


def block_program(nc, x, meta, w_pair, w_v, w_kb, consts, rope_cs, w_out, sinks, ln_ffn, fnorm,
                  w_query, keys_t, experts, out):
    with ExitStack() as ctx:
        def sb(name, words):
            return ctx.enter_context(nc.sbuf_tensor(name, [P, words], F32))

        def sem(name):
            return ctx.enter_context(nc.semaphore(name))

        def scratch(name, shape):
            return nc.dram_tensor(name, shape, F32, kind="Internal").ap()

        def parts(region, sizes):
            at, views = 0, []
            for words in sizes:
                views.append(region[:, at:at + words])
                at += words
            return views

        def grid(view, a):
            return view.rearrange("p (a n) -> p a n", a=a)

        ps = ctx.enter_context(nc.psum_tensor("ps", [P, 8, 512], F32))

        cst = sb("cst", C_ALL)
        ident = cst[:, C_ID:C_ID + P]
        negtri = cst[:, C_TRI:C_TRI + P]
        negones = cst[:, C_ONES:C_ONES + P]
        mask01 = cst[:, C_M01:C_M01 + P]
        maskneg = cst[:, C_MNEG:C_MNEG + P]
        perm = cst[:, C_PERM:C_PERM + P]
        iota = cst[:, C_IOTA:C_IOTA + NC]
        winmask = grid(cst[:, C_WM:C_WM + 2 * WIN], 2)
        mixgain = cst[:, C_GAIN:C_GAIN + 8]
        lnmix = cst[:, C_LNM:C_LNM + DC]
        sinkb = sb("sinkb", HEADS)
        lnb = sb("lnb", D)
        fnb = sb("fnb", D)
        keysT = grid(sb("keysT", PH * NKEYS), PH)

        r_uv = sb("r_uv", NB * 2 * D)
        uv = grid(r_uv[:, :], NB)
        xnT_v, vall_v, xt_v = parts(r_uv, [DC * L, (NT + 1) * VW, 2 * D])
        xnT, vall, xt = grid(xnT_v, DC), grid(vall_v, NT + 1), grid(xt_v, 2)
        r_wo = sb("r_wo", DC * D)
        wout = grid(r_wo[:, :], DC)
        wpair_v, wkb_v, xTc_v, vpair_v = parts(r_wo, [DC * QKW, DC * P, 2 * D, (NT + 1) * P])
        wpair, wkb = grid(wpair_v, DC), grid(wkb_v, DC)
        xTc = xTc_v.rearrange("p (u c n) -> p u c n", u=2, c=DC)
        vpair = grid(vpair_v, NT + 1)
        r_wq = sb("r_wq", DC * D)
        wq = grid(r_wq[:, :], DC)
        wv_v, cos, sin = parts(r_wq, [DC * VW, L, L])
        wv = grid(wv_v, DC)

        hncur = sb("hncur", D)
        h2cur = sb("h2cur", D)
        vprev = sb("vprev", P)
        kbcur = sb("kbcur", WIN)
        small = sb("small", 64)
        r_wk = sb("r_wk", 13216)
        (pT_v, ssb_v, sq_v, qT_v, hs, hnn, in_v, topv_v, topi_v, topf_v, cs_v, ci_v,
         lw1_v, tops_v, pos_v, posf_v, idxf, idxn, gn, actv, gel, idxcur, gcur, diag_v) = parts(r_wk, [
             2048, 2048, D, D, D, D, 512 + P + 512, 256, 256, 256, PH * NC, PH * NC,
             512, K, K, K, K, K, K, K, K, K, K, 4 * P])
        pT = pT_v.rearrange("p (a h n) -> p a h n", a=2, h=8)
        s_all = grid(pT_v, 2 * PH)
        ssb = grid(ssb_v[:, 0:HEADS * WIN], HEADS)
        sq = grid(sq_v, 8)
        hnT = grid(sq_v, DC)
        half = TOPK // 2 * NC
        eq_pT, eq_first = (
            [grid(view[:, at:at + half], TOPK // 2) for at in (0, step)]
            for view, step in ((pT_v, PH * NKEYS), (sq_v, half)))
        qT = grid(qT_v, PH)
        ob = grid(qT_v[:, 0:512], 4)
        qb_v, vown, oa_v = parts(in_v, [512, P, 512])
        qb = grid(qb_v, 4)
        oa = grid(oa_v, 4)
        topv, topf = grid(topv_v, 16), grid(topf_v, 16)
        topi = grid(topi_v.bitcast(U32), 16)
        cs, ci = grid(cs_v, PH), grid(ci_v, PH)
        tops, posf = grid(tops_v, PH), grid(posf_v, PH)
        pos = grid(pos_v.bitcast(U32), PH)
        idxf3, gn3, gcur3 = grid(idxf, PH), grid(gn, PH), grid(gcur, PH)
        idxn_u, idxcur_u = idxn.bitcast(U32), idxcur.bitcast(U32)
        diag = grid(diag_v, 4)
        lq, *lkv = parts(in_v, [512] + [2 * P] * 2)
        lkv += parts(sq_v, [2 * P] * (LKB - 2))
        lsp_v, lacc_v = parts(ssb_v, [2 * 512, 2 * 512])
        lsp, lacc = grid(lsp_v, 2), grid(lacc_v, 2)
        laz, lw0_v = parts(qT_v, [512, 512])
        lw = (lw0_v, lw1_v)
        (qpair, kpair, ropx, ropt, az_v, sp_v, w_v2, acc_v, oT) = parts(r_wk, [
            SEQ, L, L, L, 2 * 512, SPB * 512, 2 * 512, 2 * SEQ, SEQ])
        az, sp, wb, acc = grid(az_v, 2), grid(sp_v, SPB), grid(w_v2, 2), grid(acc_v, 2)

        nssq, nr = small[:, 0:2], small[:, 2:4]
        mx, nmx, se, rs, rden = (small[:, 4 + 8 * i:12 + 8 * i] for i in range(5))
        r2 = small[:, 44:46]
        r3 = small[:, 46:48]
        r4 = small[:, 48:50]
        gsum = small[:, 50:58]
        onecol = small[:, 58:59]
        epscol = small[:, 59:60]
        newton = small[:, 60:64]

        qb_dram = scratch("qb_dram", [P, PAIRS, SEQ])
        kb_dram = scratch("kb_dram", [P, KCOLS])
        vb_dram = scratch("vb_dram", [CHUNK + SEQ, P])
        oa_dram = scratch("oa_dram", [P, PAIRS, SEQ])
        lq_dram = scratch("lq_dram", [P, PAIRS, 512])
        lkv_dram = scratch("lkv_dram", [P, PAIRS, NT, 2 * P])
        lkm_dram = scratch("lkm_dram", [P, PAIRS, META])
        lvm_dram = scratch("lvm_dram", [META, PAIRS, P])

        consts_in, side_in, wv_in, wkb_in = sem("consts_in"), sem("side_in"), sem("wv_in"), sem("wkb_in")
        x_in = [sem("x_in0"), sem("x_in1")]
        squared, scaled, turned, xT_ready = sem("squared"), sem("scaled"), sem("turned"), sem("xT_ready")
        xT_kept, v_summed, v_kept = sem("xT_kept"), sem("v_summed"), sem("v_kept")
        zeroed, k_summed, k_kept, k_turned, k_roped = (
            sem("zeroed"), sem("k_summed"), sem("k_kept"), sem("k_turned"), sem("k_roped"))
        side_out = sem("side_out")
        wpair_in, proj_summed, proj_kept, q_turned, q_roped = (
            sem("wpair_in"), sem("proj_summed"), sem("proj_kept"), sem("q_turned"), sem("q_roped"))
        vpair_ready, qb_out, qb_free, oa_out, oT_free, oT_ready = (
            sem("vpair_ready"), sem("qb_out"), sem("qb_free"), sem("oa_out"), sem("oT_free"),
            sem("oT_ready"))
        z_ready, abs_ready, log_ready, sp_ready, tri_done, acc_ready, w_ready, w_used = (
            sem("z_ready"), sem("abs_ready"), sem("log_ready"), sem("sp_ready"), sem("tri_done"),
            sem("acc_ready"), sem("w_ready"), sem("w_used"))
        eps_set = sem("eps_set")
        lq_in, lkv_in = sem("lq_in"), [sem(f"lkv_in{i}") for i in range(LKB)]
        lz_ready, llog_ready, lsp_ready, ltri_done, lacc_ready, lw_ready, lw_used = (
            sem("lz_ready"), sem("llog_ready"), sem("lsp_ready"), sem("ltri_done"),
            sem("lacc_ready"), sem("lw_ready"), sem("lw_used"))
        lo_ready, lo_out = sem("lo_ready"), sem("lo_out")
        wout_in, wq_in = sem("wout_in"), sem("wq_in")
        wout_scaled = sem("wout_scaled")
        tile_in, score_done, max_ready, exp_ready, p_ready = (
            sem("tile_in"), sem("score_done"), sem("max_ready"), sem("exp_ready"), sem("p_ready"))
        pt_done, pt_kept_a, pt_kept_v, ob_done, ob_ready, ssq_done, r2_ready = (
            sem("pt_done"), sem("pt_kept_a"), sem("pt_kept_v"), sem("ob_done"), sem("ob_ready"),
            sem("ssq_done"), sem("r2_ready"))
        mix_done, h2_ready, h2_squared, hn_ready = (
            sem("mix_done"), sem("h2_ready"), sem("h2_squared"), sem("hn_ready"))
        hnT_done, hnT_kept, qT_done, qT_kept, key_done, key_kept = (
            sem("hnT_done"), sem("hnT_kept"), sem("qT_done"), sem("qT_kept"), sem("key_done"),
            sem("key_kept"))
        oa_in, gate_in, gate_exp, routed = sem("oa_in"), sem("gate_in"), sem("gate_exp"), sem("routed")
        head_ready, head_in, head_exp = sem("head_ready"), sem("head_in"), sem("head_exp")
        rows_in = [sem(f"rows_in{i}") for i in range(NB)]
        idx_ready, dotted, gelu_ready, diag_ready, rows_used = (
            sem("idx_ready"), sem("dotted"), sem("gelu_ready"), sem("diag_ready"), sem("rows_used"))
        h2_copied, h2_free, h3_ready, h3_squared, out_ready, out_done = (
            sem("h2_copied"), sem("h2_free"), sem("h3_ready"), sem("h3_squared"), sem("out_ready"),
            sem("out_done"))
        passed = {}
        for name in ("pe", "act", "dve", "pool", "sp"):
            passed[name] = sem("passed_" + name)

        act_own, dve_own = sem("act_own"), sem("dve_own")

        def gate(eng, name, semaphore, value):
            eng.wait_ge(semaphore, value)
            eng.sem_inc(passed[name], 1)

        N_SIDE = 4
        block = ctx.enter_context(nc.Block())

        @block.sync
        def _(sp_eng):
            e = sp_eng
            e.dma_start(xt[:, 0, :], x[0:P, :]).then_inc(x_in[0], 16)
            e.dma_start(cst[:, :], consts).then_inc(consts_in, 16)
            e.dma_start(xt[:, 1, :], x[P:2 * P, :]).then_inc(x_in[1], 16)
            e.dma_start(wv[:, :, :], w_v).then_inc(wv_in, 16)
            e.dma_start(wkb[:, :, :], w_kb).then_inc(wkb_in, 16)
            e.dma_start(r_wq[:, DC * VW:DC * VW + 2 * L], rope_cs).then_inc(wkb_in, 16)
            e.dma_start(wpair[:, :, :], w_pair[0]).then_inc(wpair_in, 16)
            with nc.sync.Fori(1, NT // 2) as m:
                for u in range(2):
                    e.wait_ge(turned, 2 * m + u - 1)
                    e.dma_start(xt[:, u, :], x[bass.ds((2 * m + u) * P, P), :]).then_inc(x_in[u], 16)
            e.wait_ge(turned, NT - 1)
            e.dma_start(xt[0:META, 0, :], meta).then_inc(x_in[0], 16)
            e.dma_start(sinkb[:, :], sinks.partition_broadcast(P)).then_inc(side_in, 16)
            e.dma_start(lnb[:, :], ln_ffn.partition_broadcast(P)).then_inc(side_in, 16)
            e.dma_start(fnb[:, :], fnorm.partition_broadcast(P)).then_inc(side_in, 16)
            e.dma_start(keysT[:, :, :], keys_t).then_inc(side_in, 16)
            e.wait_ge(zeroed, 1)
            e.dma_start(vb_dram[0:CHUNK, :], oT[0:CHUNK, 0:P]).then_inc(side_out, 16)
            e.dma_start(kb_dram[:, META:META + CHUNK], oT[:, 0:CHUNK]).then_inc(side_out, 16)
            e.wait_ge(v_kept, NT + 1 + AHEAD)
            e.dma_start(vb_dram[CHUNK:CHUNK + SEQ, :].rearrange("(n p) c -> p n c", p=P),
                        vall[:, 0:NT, HEADS * HD:VW]).then_inc(side_out, 16)
            e.dma_start(vprev[0:META, :], vall[0:META, NT, HEADS * HD:VW]).then_inc(side_out, 16)
            e.wait_ge(k_roped, 3)
            e.dma_start(kb_dram[:, META + CHUNK:KCOLS], ropx[:, 0:SEQ]).then_inc(side_out, 16)
            e.dma_start(kbcur[:, 0:META], ropx[:, SEQ:L]).then_inc(side_out, 16)
            e.wait_ge(side_out, 16 * 6)
            e.sem_inc(qb_free, 1)
            e.sem_inc(oT_free, 1)

            def pair_moves(hp, more):
                if more:
                    e.wait_ge(proj_summed, 7 * hp + 7)
                    e.dma_start(wpair[:, :, :], w_pair[bass.ds(hp + 1, 1)].rearrange("o p c n -> (o p) c n")
                                ).then_inc(wpair_in, 16)
                gate(e, "sp", proj_kept, 7 * hp + 5)
                pair = bass.ds(hp, 1)
                e.dma_start(lq_dram[:, pair, :], grid(qpair[:, 512:SEQ], 1)).then_inc(qb_out, 16)
                e.dma_start(lkv_dram[:, pair, :, 0:P].rearrange("p o j c -> p (o j) c"),
                            grid(kpair[:, 0:SEQ], NT)).then_inc(qb_out, 16)
                e.dma_start(lkm_dram[:, pair, :], grid(kpair[:, SEQ:L], 1)).then_inc(qb_out, 16)
                e.dma_start(lkv_dram[:, pair, :, P:2 * P].rearrange("p o j c -> p (o j) c"),
                            vall[:, 0:NT, bass.ds(hp * P, P)]).then_inc(qb_out, 16)
                e.dma_start(lvm_dram[:, pair, :], vall[0:META, NT:NT + 1, bass.ds(hp * P, P)]
                            ).then_inc(qb_out, 16)
                e.wait_ge(q_roped, 2 * hp + 2 + AHEAD)
                e.dma_start(qb_dram[:, bass.ds(hp, 1), :], ropx[:, 0:SEQ].rearrange("p (a n) -> p a n", a=1)
                            ).then_inc(qb_out, 16)
                e.wait_ge(qb_out, 96 * hp + 96)
                e.sem_inc(qb_free, 1)
                e.wait_ge(oT_ready, hp + 1 + 1)
                n = 512 if more else LAST_TO
                e.dma_start(oa_dram[:, bass.ds(hp, 1), 0:n], oT[:, 0:n].rearrange("p (a n) -> p a n", a=1)
                            ).then_inc(oa_out, 16)
                if more:
                    e.wait_ge(oa_out, 16 * hp + 16)
                    e.sem_inc(oT_free, 1)

            with nc.sync.Fori(0, PAIRS - 1) as hp:
                pair_moves(hp, True)
            pair_moves(PAIRS - 1, False)

            def load_tile(t):
                cols = bass.ds(t * P, P)
                e.dma_start(qb[:, :, :], qb_dram[:, :, cols]).then_inc(tile_in, 16)
                e.dma_start(kbcur[:, META:WIN], kb_dram[:, bass.ds(t * P + META, 3 * CHUNK)]).then_inc(tile_in, 16)
                e.dma_start(vprev[META:PREV, :], vb_dram[bass.ds(t * P, CHUNK), :]).then_inc(tile_in, 16)
                e.dma_start(vown[:, :], vb_dram[bass.ds(t * P + CHUNK, P), :]).then_inc(tile_in, 16)
                e.dma_start(hs[:, :], x[cols, :]).then_inc(tile_in, 16)
                if isinstance(t, int) and t == 0:
                    e.wait_ge(oa_out, 16 * PAIRS)
                e.dma_start(oa[:, :, :], oa_dram[:, :, cols]).then_inc(oa_in, 16)

            e.wait_ge(oT_ready, PAIRS + 1)
            load_tile(0)
            e.dma_start(wout[:, :, :], w_out).then_inc(wout_in, 16)
            e.dma_start(wq[:, :, :], w_query).then_inc(wq_in, 16)
            e.sem_inc(h2_free, 1)

            def late_moves(b):
                pair = bass.ds(b, 1)
                gate(e, "sp", mix_done, 4 * b + 8)
                e.dma_start(grid(lq, 1), lq_dram[:, pair, :]).then_inc(lq_in, 16)
                for i in range(NT + 1):
                    j, m = NT - 1 - i, i % LKB
                    if i == 2:
                        gate(e, "sp", qT_done, PH * b + 2 * PH)
                    if i >= LKB:
                        gate(e, "sp", lw_used, NL * b + 2 * (i - LKB + 1))
                    if i < NT:
                        e.dma_start(grid(lkv[m], 1), lkv_dram[:, pair, j:j + 1, :].rearrange("p o j c -> p (o j) c")
                                    ).then_inc(lkv_in[m], 16)
                    else:
                        e.dma_start(grid(lkv[m][:, 0:META], 1), lkm_dram[:, pair, :]).then_inc(lkv_in[m], 16)
                        e.dma_start(grid(lkv[m][0:META, P:2 * P], 1), lvm_dram[:, pair, :]
                                    ).then_inc(lkv_in[m], 16)
                gate(e, "sp", lo_ready, b + 1)
                c = late_list(b)[-1][1]
                e.dma_start(oa_dram[:, pair, c:SEQ], grid(laz[:, c - 512:512], 1)).then_inc(lo_out, 16)
                gate(e, "sp", lo_out, 16 * b + 16)

            def block_moves(b, more, late=False):
                if more:
                    e.wait_ge(h2_copied, b + 1)
                    load_tile(b + 1)
                if late:
                    late_moves(b)
                e.wait_ge(out_ready, b + 1)
                e.dma_start(out[bass.ds(b * P, P), :], h2cur[:, :]).then_inc(out_done, 16)
                e.wait_ge(out_done, 16 * b + 16)
                e.sem_inc(h2_free, 1)

            with nc.sync.Fori(0, LAST) as b:
                block_moves(b, True, True)
            block_moves(LAST, True, True)
            with nc.sync.Fori(PAIRS, NT - 1) as b:
                block_moves(b, True)
            block_moves(NT - 1, False)
            e.wait_ge(out_done, 16 * NT)

        @block.gpsimd
        def _(pool):
            g = nc.gpsimd
            pool.sem_inc(xT_kept, AHEAD)
            g.memset(oT[:, 0:P], 0.0).then_inc(zeroed, 1)

            def keep_xT(n, u, rows):
                gate(pool, "pool", xT_ready, n + 1 + AHEAD)
                g.tensor_copy(xnT[:, :, bass.ds(n * P, rows)], xTc[:, u, :, 0:rows]).then_inc(xT_kept, 1)

            with g.Fori(0, NT // 2) as m:
                for u in range(2):
                    keep_xT(2 * m + u, u, P)
            keep_xT(NT, 0, META)

            def pair(hp, units):
                ub, ab = len(EARLY) * hp, adds(EARLY) * hp
                gate(pool, "pool", proj_summed, 7 * hp + 1)
                pool.wait_ge(v_kept, NT + 1 + AHEAD)
                g.tensor_copy(vpair[:, 0:NT, :], vall[:, 0:NT, bass.ds(hp * P, P)])
                g.tensor_copy(vpair[0:META, NT, :], vall[0:META, NT, bass.ds(hp * P, P)]
                              ).then_inc(vpair_ready, 1)
                for u, (j, t0, w, h) in enumerate(units[:adds(units)]):
                    gate(pool, "pool", tri_done, ub + u + 1)
                    own = P if t0 == P * j else 0
                    if own:
                        i = g.tensor_copy(acc[:, h, t0:t0 + P], sp[:, u % SPB, 0:P])
                    if w > own:
                        i = g.tensor_tensor(acc[:, h, t0 + own:t0 + w], acc[:, h, t0 + own:t0 + w],
                                            sp[:, u % SPB, own:w], ALU.add)
                    i.then_inc(acc_ready, 1)

            with g.Fori(0, LAST) as hp:
                pair(hp, EARLY)
            pair(LAST, LAST_EARLY)

            def late_add(b, u):
                j, t0, w, h = late_list(b)[u]
                if j < NT:
                    gate(pool, "pool", ltri_done, NL * b + u + 1)
                    own, c = (P if t0 == P * j else 0), t0 - 512
                    if own:
                        i = g.tensor_copy(lacc[:, h, c:c + P], lsp[:, u % 2, 0:P])
                    if w > own:
                        i = g.tensor_tensor(lacc[:, h, c + own:c + w], lacc[:, h, c + own:c + w],
                                            lsp[:, u % 2, own:w], ALU.add)
                    i.then_inc(lacc_ready, 1)

            def gathers_of(b, late=False):
                for k in range(K):
                    if isinstance(b, int) and b == 0:
                        if k % TOPK == 0:
                            gate(pool, "pool", head_ready, k // TOPK + 1)
                    elif k % (K // 2) == 0:
                        gate(pool, "pool", idx_ready, 2 * b + k // (K // 2) + 1)
                    gate(pool, "pool", rows_used, K * b + k + 1)
                    g.indirect_dma_start(uv[:, k % NB, :], None, experts,
                                         bass.IndirectOffsetOnAxis(idxcur_u[:, k:k + 1], 0)
                                         ).then_inc(rows_in[k % NB], 16)
                    if late and k % GRP == GRP - 1:
                        for u in late_units(k // GRP - 6):
                            late_add(b, u)

            gathers_of(0, True)
            with g.Fori(1, LAST) as b:
                gathers_of(b, True)
            gathers_of(LAST, True)
            with g.Fori(PAIRS, NT) as b:
                gathers_of(b)

        @block.scalar
        def _(act):
            a = nc.scalar
            own = Own(act, act_own)
            link = own.link
            act.sem_inc(v_kept, AHEAD)
            act.sem_inc(w_ready, ZB)
            act.sem_inc(gate_exp, 1)
            act.wait_ge(consts_in, 16)

            def log_exp_table():
                act.sem_inc(passed["act"], 1)
                a.preload_act_table_set("natural_log_exp_and_others")

            def rsqrt_mean(r, sums, n):
                log_exp_table()
                link(a.activation(r, sums, ACT.Ln, scale=1.0 / n, bias=epscol[0:r.shape[0], :]))
                return a.activation(r, r, ACT.Exp, scale=-0.5)

            act.wait_ge(eps_set, 1)

            def front(n, u, rows, m):
                act.wait_ge(x_in[u], 16 * m + 16)
                link(a.activation((hncur, h2cur)[u][0:rows, :], xt[0:rows, u, :], ACT.Square,
                                  accum_out=nssq[0:rows, u:u + 1]))
                rsqrt_mean(nr[0:rows, u:u + 1], nssq[0:rows, u:u + 1], D).then_inc(squared, 1)

            def back(n, u, rows):
                act.wait_ge(v_summed, n + 1 + AHEAD)
                a.activation(vall[0:rows, bass.ds(n, 1), 0:512], ps[0:rows, 4 + 2 * u:5 + 2 * u, :], ACT.Copy)
                a.activation(vall[0:rows, bass.ds(n, 1), 512:VW], ps[0:rows, 5 + 2 * u:6 + 2 * u, 0:P], ACT.Copy
                             ).then_inc(v_kept, 1)

            front(0, 0, P, 0)
            front(1, 1, P, 0)
            own.settle()
            with a.Fori(0, NT // 2 - 1) as m:
                for u in range(2):
                    front(2 * m + 2 + u, u, P, m + 1)
                    back(2 * m + u, u, P)
                own.settle()
            front(NT, 0, META, NT // 2)
            back(NT - 2, 0, P)
            back(NT - 1, 1, P)
            back(NT, 0, META)
            for i, (c0, w) in enumerate(SPANS):
                act.wait_ge(k_summed, i + 1)
                a.activation(ropx[:, c0:c0 + w], ps[:, i, 0:w], ACT.Copy).then_inc(k_kept, 1)

            kept = ([(qpair, c0, w, QSCALE) for c0, w in SPANS[:2]] + [(kpair, c0, w, 1.0) for c0, w in SPANS]
                    + [(ropx, c0, w, QSCALE) for c0, w in SPANS[:2]])
            own.settle()
            log_exp_table()
            def pair(hp, units):
                ub, nu = len(EARLY) * hp, len(units)
                for i, (dst, c0, w, s) in enumerate(kept):
                    if i == 0:
                        gate(act, "act", qb_free, hp + 1)
                    act.wait_ge(proj_summed, 7 * hp + i + 1)
                    a.activation(dst[:, c0:c0 + w], ps[:, 4 + i % 2, 0:w], ACT.Copy, scale=s).then_inc(proj_kept, 1)

                def logs(u):
                    j, t0, w, h = units[u]
                    r = P if j < NT else META
                    act.wait_ge(abs_ready, ub + u + 1)
                    link(a.activation(az[0:r, u % 2, 0:w], az[0:r, u % 2, 0:w], ACT.Exp, scale=-1.0))
                    a.activation(az[0:r, u % 2, 0:w], az[0:r, u % 2, 0:w], ACT.Ln, bias=1.0).then_inc(log_ready, 1)

                def weights(u):
                    j, t0, w, h = units[u]
                    r = P if j < NT else META
                    gate(act, "act", w_used, ub + u + 1)
                    act.wait_ge(tri_done, ub + u + 1)
                    a.activation(wb[0:r, u % 2, 0:w], ps[0:r, u % ZB, 0:w], ACT.Exp).then_inc(w_ready, 1)

                for u in range(nu + 2):
                    if u < nu:
                        logs(u)
                    if u >= 2:
                        weights(u - 2)
                own.settle()

            with a.Fori(0, LAST) as hp:
                pair(hp, EARLY)
            pair(LAST, LAST_EARLY)

            def late_logs(b, u):
                j, t0, w, h = late_list(b)[u]
                r = P if j < NT else META
                if u >= 1:
                    gate(act, "act", lsp_ready, NL * b + u)
                act.wait_ge(lz_ready, NL * b + u + 1)
                link(a.activation(laz[0:r, 0:w], ps[0:r, 2 + u % ZB, 0:w], ACT.Abs))
                link(a.activation(laz[0:r, 0:w], laz[0:r, 0:w], ACT.Exp, scale=-1.0))
                a.activation(laz[0:r, 0:w], laz[0:r, 0:w], ACT.Ln, bias=1.0).then_inc(llog_ready, 1)

            def late_weights(b, u):
                j, t0, w, h = late_list(b)[u]
                r = P if j < NT else META
                if u >= 2:
                    gate(act, "act", lw_used, NL * b + u - 1)
                act.wait_ge(ltri_done, NL * b + u + 1)
                a.activation(lw[u % 2][0:r, 0:w], ps[0:r, 2 + u % ZB, 0:w], ACT.Exp).then_inc(lw_ready, 1)

            def tile_step(step, t):
                if step == "exp":
                    act.wait_ge(max_ready, t + 1)
                    for h in range(HEADS):
                        a.activation(ssb[:, h, :], ssb[:, h, :], ACT.Exp, bias=nmx[:, h:h + 1],
                                     accum_out=rs[:, h:h + 1])
                    a.activation(se, se, ACT.Exp).then_inc(exp_ready, 1)
                elif step == "pT":
                    for i in range(2):
                        act.wait_ge(pt_done, 4 * t + i + 1)
                        last = a.activation(pT[0:PREV, 0, 4 * i:4 * i + 4, :],
                                            grid(ps[0:PREV, 2 + i, :], 4), ACT.Copy)
                    last.then_inc(pt_kept_a, 1)
                elif step == "ob":
                    act.wait_ge(oa_in, 16 * t + 16)
                    a.activation(sq[:, 0:4, :], oa[:, :, :], ACT.Square)
                    act.wait_ge(ob_done, t + 1)
                    a.activation(sq[:, 4:8, :], grid(ps[:, 6, :], 4), ACT.Square)
                    a.activation(ob[:, :, :], grid(ps[:, 6, :], 4), ACT.Copy).then_inc(ob_ready, 1)
                elif step == "h2sq":
                    act.wait_ge(h2_ready, t + 1)
                    link(a.activation(hnn[:, :], hs[:, :], ACT.Square, accum_out=r3[:, 0:1]))
                    rsqrt_mean(r3[:, 1:2], r3[:, 0:1], D).then_inc(h2_squared, 1)
                elif step == "r2":
                    act.wait_ge(ssq_done, t + 1)
                    rsqrt_mean(r2, ps[:, 7, 0:2], HEADS * HD).then_inc(r2_ready, 1)
                elif step == "hnT":
                    for i in range(2):
                        act.wait_ge(hnT_done, 2 * t + i + 1)
                        a.activation(hnT[:, 4 * i:4 * i + 4, :], grid(ps[:, 2 + i, :], 4), ACT.Copy
                                     ).then_inc(hnT_kept, 1)
                elif step == "qT":
                    for i in range(2):
                        act.wait_ge(qT_done, PH * t + 4 * i + 4)
                        a.activation(qT[:, 4 * i:4 * i + 4, :], grid(ps[:, 4 + i, :], 4), ACT.Copy
                                     ).then_inc(qT_kept, 1)
                elif step == "keys":
                    for i, bank in enumerate(KEY_BANKS):
                        act.wait_ge(key_done, 4 * t + i + 1)
                        a.activation(s_all[:, 4 * i:4 * i + 4, :], grid(ps[:, bank, :], 4), ACT.Copy
                                     ).then_inc(key_kept, 1)
                elif step == "gexp":
                    act.wait_ge(gate_in, t + 1)
                    a.activation(gn, gn, ACT.Exp).then_inc(gate_exp, 1)

            def head_gates(h):
                act.wait_ge(head_in, h + 1)
                a.activation(gn3[:, h, :], gn3[:, h, :], ACT.Exp).then_inc(head_exp, 1)

            at = {7: "exp", 10: "pT", 13: "ob", 15: "r2", 20: "h2sq", 23: "hnT", 32: "qT", 34: "keys", 58: "gexp"}
            for step in at.values():
                if step == "gexp":
                    head_gates(0)
                else:
                    tile_step(step, 0)
                if step == "ob":
                    act.wait_ge(wout_in, 16)
                    for c in range(2 * PAIRS):
                        last = a.activation(wout[:, c, :], wout[:, c, :], ACT.Copy, scale=mixgain[:, c:c + 1])
                    last.then_inc(wout_scaled, 1)

            def experts_of(b, more, late=False):
                for n in range(NG):
                    act.wait_ge(dotted, K * b + GRP * (n + 1))
                    a.activation(gel[:, GRP * n:GRP * n + GRP], actv[:, GRP * n:GRP * n + GRP], ACT.Gelu
                                 ).then_inc(gelu_ready, 1)
                    if isinstance(b, int) and b == 0 and n - 1 in HEAD_AT:
                        head_gates(1 + HEAD_AT.index(n - 1))
                    if more and n in at:
                        tile_step(at[n], b + 1)
                    if late and (late_units(n - 4) or late_units(n - 2)):
                        log_exp_table()
                        for u in late_units(n - 4):
                            late_weights(b, u)
                        for u in late_units(n - 2):
                            late_logs(b, u)
                act.wait_ge(h3_ready, b + 1 + 1)
                link(a.activation(hncur[:, :], h2cur[:, :], ACT.Square, accum_out=r4[:, 0:1]))
                rsqrt_mean(r4[:, 1:2], r4[:, 0:1], D).then_inc(h3_squared, 1)

            own.settle()
            experts_of(0, True, True)
            own.settle()
            with a.Fori(1, LAST) as b:
                experts_of(b, True, True)
                own.settle()
            experts_of(LAST, True, True)
            own.settle()
            with a.Fori(PAIRS, NT - 1) as b:
                experts_of(b, True)
                own.settle()
            experts_of(NT - 1, False)

        @block.vector
        def _(dve):
            v = nc.vector
            own = Own(dve, dve_own)
            link = own.link
            dve.sem_inc(xT_ready, AHEAD)
            dve.sem_inc(q_roped, AHEAD)
            dve.sem_inc(oT_ready, 1)
            dve.sem_inc(routed, 2)
            dve.sem_inc(idx_ready, 2)
            dve.sem_inc(gate_in, 1)
            dve.sem_inc(h3_ready, 1)
            v.memset(onecol, 1.0)
            v.memset(epscol, EPS).then_inc(eps_set, 1)
            dve.wait_ge(consts_in, 16)

            def polish(r, sums, n):
                rows, w = r.shape
                m, q = (newton[0:rows, w * i:w * i + w] for i in range(2))
                v.tensor_scalar(m, sums, 1.0 / n, EPS, ALU.mult, ALU.add)
                link(v.tensor_tensor(q, r, r, ALU.mult))
                link(v.tensor_tensor(q, q, m, ALU.mult))
                link(v.tensor_scalar(q, q, -0.5, 1.5, ALU.mult, ALU.add))
                link(v.tensor_tensor(r, r, q, ALU.mult))

            def front(n, u, rows):
                dve.wait_ge(squared, n + 1)
                polish(nr[0:rows, u:u + 1], nssq[0:rows, u:u + 1], D)
                v.tensor_scalar(xt[0:rows, u, :], xt[0:rows, u, :], nr[0:rows, u:u + 1], None, ALU.mult
                                ).then_inc(scaled, 1)

            def back(n, u, rows):
                dve.wait_ge(xT_kept, n + 1)
                dve.wait_ge(v_summed, n + 1)
                dve.wait_ge(turned, n + 1)
                for c in range(0, DC, 4):
                    last = v.tensor_tensor(
                        xTc[:, u, c:c + 4, 0:rows], grid(ps[:, 2 * u + c // 4, :], 4)[:, :, 0:rows],
                        lnmix[:, c:c + 4].unsqueeze(2).to_broadcast([P, 4, rows]), ALU.mult)
                last.then_inc(xT_ready, 1)

            front(0, 0, P)
            own.settle()
            with v.Fori(0, NT // 2 - 1) as m:
                front(2 * m + 1, 1, P)
                back(2 * m, 0, P)
                front(2 * m + 2, 0, P)
                back(2 * m + 1, 1, P)
                own.settle()
            front(NT - 1, 1, P)
            back(NT - 2, 0, P)
            front(NT, 0, META)
            back(NT - 1, 1, P)
            back(NT, 0, META)

            def rotate(bank, c0, w):
                cols = slice(c0, c0 + w)
                v.tensor_tensor(ropt[:, cols], ps[:, bank, 0:w], sin[:, cols], ALU.mult)
                link(v.tensor_tensor(ropx[:, cols], ropx[:, cols], cos[:, cols], ALU.mult))
                return v.tensor_tensor(ropx[:, cols], ropx[:, cols], ropt[:, cols], ALU.add)

            for i, (c0, w) in enumerate(SPANS):
                dve.wait_ge(k_turned, i + 1)
                rotate(3 + i, c0, w).then_inc(k_roped, 1)

            own.settle()
            def pair(hp, units):
                ub, ab, nu = len(EARLY) * hp, adds(EARLY) * hp, len(units)
                for i, (c0, w) in enumerate(SPANS[:2]):
                    dve.wait_ge(q_turned, 2 * hp + i + 1)
                    rotate(4 + i, c0, w).then_inc(q_roped, 1)

                def magnitude(u):
                    j, t0, w, h = units[u]
                    r = P if j < NT else META
                    if u >= 2:
                        dve.wait_ge(sp_ready, ub + u - 1)
                    dve.wait_ge(z_ready, ub + u + 1)
                    v.tensor_scalar(az[0:r, u % 2, 0:w].bitcast(U32), ps[0:r, u % ZB, 0:w].bitcast(U32),
                                    0x7FFFFFFF, None, ALU.bitwise_and).then_inc(abs_ready, 1)

                def softplus(u):
                    j, t0, w, h = units[u]
                    r = P if j < NT else META
                    if u >= SPB:
                        dve.wait_ge(acc_ready, ab + min(u - SPB + 1, adds(units)))
                    dve.wait_ge(log_ready, ub + u + 1)
                    i = v.scalar_tensor_tensor(out=sp[0:r, u % SPB, 0:w], in0=ps[0:r, u % ZB, 0:w], scalar=0.0,
                                               in1=az[0:r, u % 2, 0:w], op0=ALU.max, op1=ALU.add)
                    if t0 == P * j:
                        link(i)
                        i = v.tensor_tensor(sp[:, u % SPB, 0:P], sp[:, u % SPB, 0:P], mask01, ALU.mult)
                    i.then_inc(sp_ready, 1)

                for u in range(nu + 1):
                    if u < nu:
                        magnitude(u)
                    if u >= 1:
                        softplus(u - 1)
                dve.wait_ge(oT_free, hp + 1)
                dve.wait_ge(w_used, ub + nu + AHEAD)
                last = v.tensor_copy(oT[:, 0:512], ps[:, 6, :])
                if units is LAST_EARLY:
                    last = v.tensor_copy(oT[:, 512:LAST_TO], ps[:, 7, 0:LAST_TO - 512])
                last.then_inc(oT_ready, 1)
                own.settle()

            with v.Fori(0, LAST) as hp:
                pair(hp, EARLY)
            pair(LAST, LAST_EARLY)

            def late_softplus(b, u):
                j, t0, w, h = late_list(b)[u]
                r = P if j < NT else META
                if u >= 2:
                    dve.wait_ge(lacc_ready, NLADD * b + u - 1)
                dve.wait_ge(llog_ready, NL * b + u + 1)
                i = v.scalar_tensor_tensor(out=lsp[0:r, u % 2, 0:w], in0=ps[0:r, 2 + u % ZB, 0:w], scalar=0.0,
                                           in1=laz[0:r, 0:w], op0=ALU.max, op1=ALU.add)
                if t0 == P * j:
                    link(i)
                    i = v.tensor_tensor(lsp[:, u % 2, 0:P], lsp[:, u % 2, 0:P], mask01, ALU.mult)
                i.then_inc(lsp_ready, 1)

            def top16(values, places, scores, rows):
                for row in rows:
                    last = v.max(values[:, row, 0:8], scores[:, row, :])
                link(last)
                for row in rows:
                    last = v.max_index(places[:, row, 0:8], values[:, row, 0:8], scores[:, row, :])
                link(last)
                for row in rows:
                    last = v.match_replace(scores[:, row, :], values[:, row, 0:8], scores[:, row, :], -3e38)
                link(last)
                for row in rows:
                    last = v.max(values[:, row, 8:16], scores[:, row, :])
                link(last)
                for row in rows:
                    last = v.max_index(places[:, row, 8:16], values[:, row, 8:16], scores[:, row, :])
                link(last)

            dve.wait_ge(side_in, 16 * N_SIDE)

            def tile_step(step, t):
                if step == "mask":
                    dve.wait_ge(score_done, t + 1)
                    m = winmask[:, 0 if isinstance(t, int) and t == 0 else 1, :]
                    for i in range(4):
                        last = v.tensor_tensor(ssb[:, 2 * i:2 * i + 2, :], grid(ps[:, 2 + i, 0:2 * WIN], 2),
                                               m.unsqueeze(1).to_broadcast([P, 2, WIN]), ALU.add)
                    link(last)
                    link(v.tensor_reduce(mx, ssb[:, :, :], AX.X, ALU.max))
                    link(v.tensor_tensor(mx, mx, sinkb[:, :], ALU.max))
                    v.tensor_tensor(se, sinkb[:, :], mx, ALU.subtract)
                    v.tensor_scalar(nmx, mx, -1.0, None, ALU.mult).then_inc(max_ready, 1)
                elif step == "norm":
                    dve.wait_ge(exp_ready, t + 1)
                    link(v.tensor_tensor(rden, rs, se, ALU.add))
                    link(v.reciprocal(rden, rden))
                    v.tensor_tensor(ssb[:, :, :], ssb[:, :, :], rden.unsqueeze(2).to_broadcast([P, HEADS, WIN]),
                                    ALU.mult).then_inc(p_ready, 1)
                elif step == "pT":
                    for i in range(2):
                        dve.wait_ge(pt_done, 4 * t + i + 3)
                        last = v.tensor_copy(pT[:, 1, 4 * i:4 * i + 4, :], grid(ps[:, 4 + i, :], 4))
                    last.then_inc(pt_kept_v, 1)
                elif step == "r2":
                    dve.wait_ge(r2_ready, t + 1)
                    polish(r2, ps[:, 7, 0:2], HEADS * HD)
                elif step == "h2":
                    dve.wait_ge(mix_done, 4 * t + 4)
                    hg = grid(hs, 2)
                    link(v.scalar_tensor_tensor(out=hg, in0=ps[:, 2:4, :], scalar=r2[:, 0:1], in1=hg,
                                                op0=ALU.mult, op1=ALU.add))
                    v.scalar_tensor_tensor(out=hg, in0=ps[:, 4:6, :], scalar=r2[:, 1:2], in1=hg,
                                           op0=ALU.mult, op1=ALU.add).then_inc(h2_ready, 1)
                elif step == "hn":
                    dve.wait_ge(h2_squared, t + 1)
                    polish(r3[:, 1:2], r3[:, 0:1], D)
                    v.scalar_tensor_tensor(out=hnn, in0=hs, scalar=r3[:, 1:2], in1=lnb[:, :],
                                           op0=ALU.mult, op1=ALU.mult).then_inc(hn_ready, 1)
                elif step[0] == "cands":
                    heads = slice(4 * step[1], 4 * step[1] + 4)
                    second = slice(PH + 4 * step[1], PH + 4 * step[1] + 4)
                    v.tensor_copy(topf[:, second, :], topi[:, second, :])
                    link(v.tensor_copy(topf[:, heads, :], topi[:, heads, :]))
                    link(v.tensor_scalar(topf[:, heads, :], topf[:, heads, :], float(NKEYS), None, ALU.mult))
                    for both, into in ((topv, cs), (topf, ci)):
                        for a0, na, nb, at in SEGS:
                            last = v.tensor_tensor(
                                into[:, heads, at:at + na * nb].rearrange("p h (a b) -> p h a b", a=na),
                                both[:, heads, a0:a0 + na].unsqueeze(3).to_broadcast([P, 4, na, nb]),
                                both[:, second, 0:nb].unsqueeze(2).to_broadcast([P, 4, na, nb]), ALU.add)
                    link(last)
                elif step == "gate":
                    v.tensor_tensor(gn3, tops[:, :, :], tops[:, :, 0:1].to_broadcast([P, PH, TOPK]),
                                    ALU.subtract).then_inc(gate_in, 1)
                    link(v.tensor_copy(idxn_u, idxf))
                elif step == "routed":
                    dve.wait_ge(gate_exp, t + 1)
                    link(v.tensor_reduce(gsum, gn3, AX.X, ALU.add))
                    link(v.reciprocal(gsum, gsum))
                    v.tensor_tensor(gn3, gn3, gsum.unsqueeze(2).to_broadcast([P, PH, TOPK]), ALU.mult
                                    ).then_inc(routed, 1)
                    v.tensor_copy(idxcur_u[:, 0:K // 2], idxn_u[:, 0:K // 2]).then_inc(idx_ready, 1)
                elif step[0] == "top":
                    if step[1] == 0:
                        gate(dve, "dve", key_kept, 4 * t + 4)
                    top16(topv, topi, s_all, (step[1], PH + step[1]))
                elif step[0] == "pick":
                    h = step[1]
                    eq = eq_first if isinstance(t, int) and t == 0 else eq_pT
                    top16(tops, pos, cs, (h,))
                    link(v.tensor_copy(posf[:, h, :], pos[:, h, :]))
                    for k in range(TOPK):
                        last = v.scalar_tensor_tensor(out=eq[2 * k // TOPK][:, k % (TOPK // 2), :], in0=iota, scalar=posf[:, h, k:k + 1],
                                                      in1=ci[:, h, :], op0=ALU.is_equal, op1=ALU.mult,
                                                      accum_out=idxf3[:, h, k:k + 1])
                    link(last)

            at = {6: "mask", 8: "norm", 11: "pT", 16: "r2", 19: "h2", 21: "hn", 40: ("cands", 0),
                  49: ("cands", 1), 57: "gate", 59: "routed"}
            for h in range(4):
                at.update({36 + h: ("top", h), 41 + 2 * h: ("pick", h), 42 + 2 * h: ("top", 4 + h),
                           50 + 2 * h: ("pick", 4 + h)})

            def head_experts(h):
                tile_step(("pick", h), 0)
                v.tensor_copy(idxcur_u[:, TOPK * h:TOPK * h + TOPK], idxf3[:, h, :]).then_inc(head_ready, 1)
                v.tensor_tensor(gn3[:, h, :], tops[:, h, :], tops[:, h, 0:1].to_broadcast([P, TOPK]),
                                ALU.subtract).then_inc(head_in, 1)

            def head_gates(h):
                dve.wait_ge(head_exp, h + 1)
                link(v.tensor_reduce(gsum[:, h:h + 1], gn3[:, h, :], AX.X, ALU.add))
                link(v.reciprocal(gsum[:, h:h + 1], gsum[:, h:h + 1]))
                link(v.tensor_scalar(gcur3[:, h, :], gn3[:, h, :], gsum[:, h:h + 1], None, ALU.mult))

            for n in sorted(at):
                if at[n] == ("pick", 0):
                    head_experts(0)
                elif at[n][0] != "pick" and at[n] not in ("gate", "routed"):
                    tile_step(at[n], 0)
            link(v.tensor_copy(hncur[:, :], hnn))
            head_gates(0)

            def experts_of(b, more, late=False):
                first = isinstance(b, int) and b == 0
                if not first:
                    v.tensor_copy(idxcur_u[:, K // 2:K], idxn_u[:, K // 2:K]).then_inc(idx_ready, 1)
                    v.tensor_copy(hncur[:, :], hnn)
                    dve.wait_ge(routed, b + 1 + 1)
                    link(v.tensor_copy(gcur, gn))
                for n in range(NG + 1):
                    if n < NG:
                        for k in range(GRP * n, GRP * n + GRP):
                            dve.wait_ge(rows_in[k % NB], (16 * K // NB) * b + 16 * (k // NB + 1))
                            v.tensor_tensor_reduce(uv[:, k % NB, 0:D], uv[:, k % NB, 0:D], hncur[:, :], 1.0, 0.0,
                                                   ALU.mult, ALU.add, actv[:, k:k + 1]).then_inc(dotted, 1)
                    if n == 2:
                        dve.wait_ge(h2_free, b + 1)
                        v.tensor_copy(h2cur[:, :], hs).then_inc(h2_copied, 1)
                    if n > 0:
                        m = n - 1
                        dve.wait_ge(rows_used, K * b + GRP * m + GRP - 4 + NB)
                        dve.wait_ge(gelu_ready, NG * b + m + 1)
                        for k in range(GRP * m, GRP * m + GRP):
                            v.tensor_scalar(diag[:, k % 4, :], ident, gel[:, k:k + 1], gcur[:, k:k + 1],
                                            ALU.mult, ALU.mult).then_inc(diag_ready, 1)
                    if late:
                        for u in late_units(n - 3):
                            late_softplus(b, u)
                        if n == LATE_AT[-1] + 6:
                            dve.wait_ge(lw_used, NL * b + NL)
                            c = late_list(b)[-1][1] - 512
                            v.tensor_copy(laz[:, c:512], ps[:, 6, c:512]).then_inc(lo_ready, 1)
                    if first and n in HEAD_AT:
                        head_experts(1 + HEAD_AT.index(n))
                    if first and n - 2 in HEAD_AT:
                        head_gates(1 + HEAD_AT.index(n - 2))
                    if more and n in at:
                        tile_step(at[n], b + 1)
                dve.wait_ge(rows_used, K * b + K + NB)
                hg = h2cur[:, :].rearrange("p (a n) -> p a n", a=2)
                v.tensor_tensor(hg, ps[:, 0:2, :], hg, ALU.add).then_inc(h3_ready, 1)
                dve.wait_ge(h3_squared, b + 1)
                polish(r4[:, 1:2], r4[:, 0:1], D)
                v.scalar_tensor_tensor(out=h2cur[:, :], in0=h2cur[:, :], scalar=r4[:, 1:2], in1=fnb[:, :],
                                       op0=ALU.mult, op1=ALU.mult).then_inc(out_ready, 1)

            own.settle()
            experts_of(0, True, True)
            own.settle()
            with v.Fori(1, LAST) as b:
                experts_of(b, True, True)
                own.settle()
            experts_of(LAST, True, True)
            own.settle()
            with v.Fori(PAIRS, NT - 1) as b:
                experts_of(b, True)
                own.settle()
            experts_of(NT - 1, False)

        @block.tensor
        def _(pe):
            t_ = nc.tensor
            pe.sem_inc(v_summed, AHEAD)
            pe.sem_inc(w_used, AHEAD)
            pe.sem_inc(rows_used, NB)
            pe.wait_ge(consts_in, 16)

            def front(n, u, rows):
                pe.wait_ge(xT_ready, n + 1)
                pe.wait_ge(scaled, n + 1)
                for c in range(DC):
                    last = t_.transpose(ps[:, 2 * u + c // 4, P * (c % 4):P * (c % 4) + rows],
                                        xt[0:rows, u, P * c:P * c + P], ident[0:rows, 0:rows])
                last.then_inc(turned, 1)

            def back(n, u, rows):
                pe.wait_ge(v_kept, n + 1)
                pe.wait_ge(xT_ready, n + 1 + AHEAD)
                for bank, c0, w in ((4 + 2 * u, 0, 512), (5 + 2 * u, 512, P)):
                    for c in range(DC):
                        last = t_.matmul(ps[0:rows, bank, 0:w], xTc[:, u, c, 0:rows], wv[:, c, c0:c0 + w],
                                         start=c == 0, stop=c == DC - 1)
                last.then_inc(v_summed, 1)

            front(0, 0, P)
            pe.wait_ge(wv_in, 16)
            with t_.Fori(0, NT // 2 - 1) as m:
                front(2 * m + 1, 1, P)
                back(2 * m, 0, P)
                front(2 * m + 2, 0, P)
                back(2 * m + 1, 1, P)
            front(NT - 1, 1, P)
            back(NT - 2, 0, P)
            front(NT, 0, META)
            back(NT - 1, 1, P)
            back(NT, 0, META)

            pe.wait_ge(wkb_in, 32)
            pe.wait_ge(xT_kept, NT + 1 + AHEAD)
            for i, (c0, w) in enumerate(SPANS):
                for c in range(DC):
                    last = t_.matmul(ps[:, i, 0:w], wkb[:, c, :], xnT[:, c, c0:c0 + w], start=c == 0,
                                     stop=c == DC - 1)
                last.then_inc(k_summed, 1)
            pe.wait_ge(v_kept, NT + 1 + AHEAD)
            for i, (c0, w) in enumerate(SPANS):
                pe.wait_ge(k_kept, i + 1)
                t_.matmul(ps[:, 3 + i, 0:w], perm, ropx[:, c0:c0 + w], start=True, stop=True).then_inc(k_turned, 1)
            pe.wait_ge(k_roped, len(SPANS))

            proj = ([(0, c0, w) for c0, w in SPANS[:2]] + [(P, c0, w) for c0, w in SPANS]
                    + [(2 * P, c0, w) for c0, w in SPANS[:2]])
            def pair(hp, units):
                ub, ab, nu = len(EARLY) * hp, adds(EARLY) * hp, len(units)
                for i, (col, c0, w) in enumerate(proj):
                    if i == 0:
                        pe.wait_ge(wpair_in, 16 * hp + 16)
                        pe.wait_ge(q_roped, 2 * hp + AHEAD)
                    if i >= 2:
                        pe.wait_ge(proj_kept, 7 * hp + i - 1)
                    for c in range(DC):
                        last = t_.matmul(ps[:, 4 + i % 2, 0:w], wpair[:, c, col:col + P], xnT[:, c, c0:c0 + w],
                                         start=c == 0, stop=c == DC - 1)
                    last.then_inc(proj_summed, 1)
                pe.wait_ge(proj_kept, 7 * hp + 7)
                for i, (c0, w) in enumerate(SPANS[:2]):
                    t_.matmul(ps[:, 4 + i, 0:w], perm, ropx[:, c0:c0 + w], start=True, stop=True
                              ).then_inc(q_turned, 1)

                def scores(u):
                    j, t0, w, h = units[u]
                    r = P if j < NT else META
                    rows = slice(HD * h, HD * h + HD)
                    gate(pe, "pe", w_ready, ub + (u + 1 if u >= ZB else ZB))
                    t_.matmul(ps[0:r, u % ZB, 0:w], kpair[rows, P * j:P * j + r], qpair[rows, t0:t0 + w],
                              start=True, stop=False, skip_group_check=True).then_inc(z_ready, 1)

                def later(u):
                    j, t0, w, h = units[u]
                    r = P if j < NT else META
                    own = P if t0 == P * j else 0
                    last_add = max([p for p in range(min(u, adds(units))) if units[p][3] == h
                                    and units[p][1] < t0 + w and t0 < units[p][1] + units[p][2]] + [-1])
                    gate(pe, "pe", sp_ready, ub + u + 1)
                    if w > own:
                        gate(pe, "pe", acc_ready, ab + last_add + 1)
                    last = t_.matmul(ps[0:r, u % ZB, 0:w], negtri[0:r, 0:r], sp[0:r, u % SPB, 0:w], start=False,
                                     stop=not own and w == own, skip_group_check=True)
                    if own:
                        last = t_.matmul(ps[:, u % ZB, 0:P], ident, maskneg, start=False, stop=w == own,
                                         skip_group_check=True)
                    if w > own:
                        last = t_.matmul(ps[0:r, u % ZB, own:w], negones[:, 0:r], acc[:, h, t0 + own:t0 + w],
                                         start=False, stop=True, skip_group_check=True)
                    last.then_inc(tri_done, 1)

                def weigh(u):
                    j, t0, w, h = units[u]
                    r = P if j < NT else META
                    first = not any(x[3] == h and x[1] // 512 == t0 // 512 for x in units[:u])
                    gate(pe, "pe", w_ready, ub + u + 1 + ZB)
                    t_.matmul(ps[HD * h:HD * h + HD, 6 + t0 // 512, t0 % 512:t0 % 512 + w],
                              vpair[0:r, j, HD * h:HD * h + HD], wb[0:r, u % 2, 0:w], start=first,
                              stop=j == NT, skip_group_check=True).then_inc(w_used, 1)

                for u in range(nu + 3):
                    if u < nu:
                        scores(u)
                    if 2 <= u < nu + 2:
                        later(u - 2)
                    if u == 3:
                        pe.wait_ge(vpair_ready, hp + 1)
                        pe.wait_ge(oT_ready, hp + 1)
                    if u >= 3:
                        weigh(u - 3)

            with t_.Fori(0, LAST) as hp:
                pair(hp, EARLY)
            pair(LAST, LAST_EARLY)
            pe.wait_ge(oT_ready, PAIRS + 1)

            def late_scores(b, u):
                j, t0, w, h = late_list(b)[u]
                i, r, c = NT - 1 - j if j < NT else NT, (P if j < NT else META), t0 - 512
                rows = slice(HD * h, HD * h + HD)
                if u == 0:
                    gate(pe, "pe", key_kept, 4 * b + 8)
                    gate(pe, "pe", lq_in, 16 * b + 16)
                if h == 0:
                    each = [1 + (k == NT) for k in range(i % LKB, NT + 1, LKB)]
                    gate(pe, "pe", lkv_in[i % LKB], 16 * sum(each) * b + 16 * sum(each[:i // LKB + 1]))
                if u >= ZB:
                    gate(pe, "pe", lw_ready, NL * b + u - ZB + 1)
                t_.matmul(ps[0:r, 2 + u % ZB, 0:w], lkv[i % LKB][rows, 0:r], lq[rows, c:c + w], start=True,
                          stop=False, skip_group_check=True).then_inc(lz_ready, 1)

            def late_later(b, u):
                j, t0, w, h = late_list(b)[u]
                r, c = (P if j < NT else META), t0 - 512
                own = P if t0 == P * j else 0
                bank = 2 + u % ZB
                gate(pe, "pe", lsp_ready, NL * b + u + 1)
                if w > own:
                    last_add = max(p for p in range(min(u, NLADD)) if late_list(b)[p][3] == h)
                    gate(pe, "pe", lacc_ready, NLADD * b + last_add + 1)
                last = t_.matmul(ps[0:r, bank, 0:w], negtri[0:r, 0:r], lsp[0:r, u % 2, 0:w], start=False,
                                 stop=not own and w == own, skip_group_check=True)
                if own:
                    last = t_.matmul(ps[:, bank, 0:P], ident, maskneg, start=False, stop=w == own,
                                     skip_group_check=True)
                if w > own:
                    last = t_.matmul(ps[0:r, bank, own:w], negones[:, 0:r], lacc[:, h, c + own:c + w],
                                     start=False, stop=True, skip_group_check=True)
                last.then_inc(ltri_done, 1)

            def late_weigh(b, u):
                j, t0, w, h = late_list(b)[u]
                i, r, c = NT - 1 - j if j < NT else NT, (P if j < NT else META), t0 - 512
                gate(pe, "pe", lw_ready, NL * b + u + 1)
                t_.matmul(ps[HD * h:HD * h + HD, 6, c:c + w], lkv[i % LKB][0:r, P + HD * h:P + HD * h + HD],
                          lw[u % 2][0:r, 0:w], start=u < 2, stop=j == NT, skip_group_check=True
                          ).then_inc(lw_used, 1)

            pe.wait_ge(side_in, 16 * N_SIDE)

            def tile_step(step, t):
                if step == "scores":
                    pe.wait_ge(routed, t + 1)
                    pe.wait_ge(tile_in, 80 * t + 80)
                    for c in range(4):
                        for h in range(2):
                            rows = slice(HD * h, HD * h + HD)
                            last = t_.matmul(ps[:, 2 + 2 * h + c // 2, WIN * (c % 2):WIN * (c % 2) + WIN],
                                             qb[rows, c, :], kbcur[rows, :], start=True, stop=True)
                    last.then_inc(score_done, 1)
                elif step == "pT":
                    pe.wait_ge(p_ready, t + 1)
                    for own, w in ((0, PREV), (1, P)):
                        for i in range(2):
                            for h in range(4):
                                last = t_.transpose(ps[0:w, 2 + 2 * own + i, P * h:P * h + P],
                                                    ssb[:, 4 * i + h, PREV * own:PREV * own + w], ident)
                            last.then_inc(pt_done, 1)
                elif step == "pv":
                    pe.wait_ge(pt_kept_a, t + 1)
                    pe.wait_ge(pt_kept_v, t + 1)
                    for h in range(2):
                        cols = slice(HD * h, HD * h + HD)
                        t_.matmul(ps[cols, 6, :], vprev[0:PREV, cols], pT[0:PREV, 0, 4 * h:4 * h + 4, :],
                                  start=True, stop=False)
                        last = t_.matmul(ps[cols, 6, :], vown[:, cols], pT[:, 1, 4 * h:4 * h + 4, :],
                                         start=False, stop=True)
                    last.then_inc(ob_done, 1)
                elif step == "ssq":
                    pe.wait_ge(ob_ready, t + 1)
                    for i in range(8):
                        last = t_.matmul(ps[:, 7, i // 4:i // 4 + 1], sq[:, i, :], onecol, start=i % 4 == 0,
                                         stop=i % 4 == 3)
                    last.then_inc(ssq_done, 1)
                elif step[0] == "mix":
                    i = step[1]
                    pe.wait_ge(wout_scaled, 1)
                    for c in range(4):
                        last = t_.matmul(ps[:, 2 + i, :], (oa, ob)[i // 2][:, c, :],
                                         wout[:, 4 * (i // 2) + c, 512 * (i % 2):512 * (i % 2) + 512],
                                         start=c == 0, stop=c == 3)
                    last.then_inc(mix_done, 1)
                elif step == "hnT":
                    pe.wait_ge(hn_ready, t + 1)
                    for c in range(DC):
                        last = t_.transpose(ps[:, 2 + c // 4, P * (c % 4):P * (c % 4) + P], hnn[:, P * c:P * c + P],
                                            ident)
                        if c % 4 == 3:
                            last.then_inc(hnT_done, 1)
                elif step[0] == "query":
                    h = step[1]
                    if h == 0:
                        pe.wait_ge(wq_in, 16)
                        pe.wait_ge(hnT_kept, 2 * t + 2)
                    for c in range(DC):
                        last = t_.matmul(ps[:, 4 + h // 4, P * (h % 4):P * (h % 4) + P], wq[:, c, P * h:P * h + P],
                                         hnT[:, c, :], start=c == 0, stop=c == DC - 1)
                    last.then_inc(qT_done, 1)
                elif step == "keys":
                    pe.wait_ge(qT_kept, 2 * t + 2)
                    for i, bank in enumerate(KEY_BANKS):
                        rows = slice(HD * (i // 2), HD * (i // 2) + HD)
                        for h in range(4):
                            last = t_.matmul(ps[:, bank, P * h:P * h + P], qT[rows, 4 * (i % 2) + h, :],
                                             keysT[rows, 4 * (i % 2) + h, :], start=True, stop=True)
                        last.then_inc(key_done, 1)

            at = {4: "scores", 9: "pT", 12: "pv", 13: "ssq", 22: "hnT", 33: "keys"}
            at.update({14 + i: ("mix", i) for i in range(4)})
            at.update({24 + i: ("query", i) for i in range(PH)})
            for n in sorted(at):
                tile_step(at[n], 0)

            def experts_of(b, more, late=False):
                for n in range(NG):
                    for k in range(GRP * n, GRP * n + GRP):
                        if k == 0:
                            pe.wait_ge(h3_ready, b + 1)
                        pe.wait_ge(diag_ready, K * b + k + 1)
                        for i in range(2):
                            last = t_.matmul(ps[:, i, :], diag[:, k % 4, :],
                                             uv[:, k % NB, D + 512 * i:D + 512 * i + 512], start=k == 0,
                                             stop=k == K - 1)
                        last.then_inc(rows_used, 1)
                    if more and n in at:
                        tile_step(at[n], b + 1)
                    if late:
                        for u in late_units(n - 2):
                            late_later(b, u)
                        for u in late_units(n - 4):
                            late_weigh(b, u)
                        for u in late_units(n):
                            late_scores(b, u)

            with t_.Fori(0, LAST) as b:
                experts_of(b, True, True)
            experts_of(LAST, True, True)
            with t_.Fori(PAIRS, NT - 1) as b:
                experts_of(b, True)
            experts_of(NT - 1, False)


def constants():
    f = np.float32
    s, t = np.arange(P)[:, None], np.arange(P)[None, :]
    c = np.zeros((P, C_ALL), f)
    c[:, C_ID:C_ID + P] = s == t
    c[:, C_TRI:C_TRI + P] = -(s >= t).astype(f)
    c[:, C_ONES:C_ONES + P] = -1
    c[:, C_M01:C_M01 + P] = s < t
    c[:, C_MNEG:C_MNEG + P] = np.where(s < t, 0, NEG)
    c[:, C_PERM:C_PERM + P] = s == (t // HD) * HD + (t + HD // 2) % HD
    c[:, C_IOTA:C_IOTA + NC] = np.arange(NC)
    part = np.concatenate([[0] * META, [1] * CHUNK, [2] * CHUNK, [3] * CHUNK])[None, :]
    chunk = s // CHUNK
    seen = (part == 0) | (part == 1 + chunk) | (part == 2 + chunk)
    c[:, C_WM:C_WM + WIN] = np.where(seen & (part != 1), 0, NEG)
    c[:, C_WM + WIN:C_WM + 2 * WIN] = np.where(seen, 0, NEG)
    return c


def rope_table():
    f = np.float32
    half = HD // 2
    freq = f(10000.0) ** (-np.arange(half, dtype=f) / f(half))
    position = np.concatenate([np.arange(META, L), np.arange(META)]).astype(f)
    angle = (position[None, :] * np.tile(freq, P // half)[:, None]).astype(f)
    sign = np.where(np.arange(P) % HD < half, f(-1), f(1))[:, None]
    return np.concatenate([np.cos(angle), sign * np.sin(angle)], axis=1).astype(f)


def kernel(x, meta_tokens, ln_mix, w_in, sb_out_norm, swa_out_norm, sinks, w_out, ln_ffn, peer_query,
           peer_sub_keys, expert_u, expert_v, final_norm):
    from concourse import bacc
    from concourse.bass_utils import run_bass_kernel_spmd

    def rows(w):
        return w.reshape(-1, P, w.shape[-1]).transpose(1, 0, 2)

    w_in, w_out = np.asarray(w_in)[0], np.asarray(w_out)[0]
    width = HEADS * HD
    order = np.arange(width).reshape(2, PAIRS, HD).transpose(1, 0, 2).reshape(-1)
    qa, ka, va, qb, kb, vb = np.split(w_in, [width, 2 * width, 3 * width, 4 * width, 4 * width + P], axis=1)
    qb = qb[:, order]
    w_pair = np.stack([rows(np.concatenate([m[:, P * i:P * i + P] for m in (qa, ka, qb)], axis=1))
                       for i in range(PAIRS)])
    w_out = np.concatenate([w_out[:width], w_out[width:][order]])
    gains = np.concatenate([np.asarray(sb_out_norm)[0], np.asarray(swa_out_norm)[0][order]])
    consts = constants()
    consts[:, C_GAIN:C_GAIN + 8] = gains.reshape(8, P).T
    consts[:, C_LNM:C_LNM + DC] = np.asarray(ln_mix)[0].reshape(DC, P).T
    keys_t = np.asarray(peer_sub_keys)[0].transpose(1, 3, 0, 2).reshape(P, PH, NKEYS)
    given = [
        ("x", np.asarray(x)[0]), ("meta", np.asarray(meta_tokens)), ("w_pair", w_pair),
        ("w_v", rows(np.concatenate([va, vb], axis=1))), ("w_kb", rows(kb)), ("consts", consts),
        ("rope_cs", rope_table()), ("w_out", rows(w_out)), ("sinks", np.asarray(sinks)[0]),
        ("ln_ffn", np.asarray(ln_ffn)[0]), ("fnorm", np.asarray(final_norm)),
        ("w_query", rows(np.asarray(peer_query)[0])), ("keys_t", keys_t),
        ("experts", np.concatenate([np.asarray(expert_u)[0], np.asarray(expert_v)[0]], axis=1)),
    ]
    nc = bacc.Bacc("TRN2", target_bir_lowering=False, num_devices=1)
    arrays, args = {}, []
    for name, array in given:
        arrays["in_" + name] = np.ascontiguousarray(array)
        args.append(nc.dram_tensor("in_" + name, array.shape, F32, kind="ExternalInput").ap())
    out = nc.dram_tensor("result", (SEQ, D), F32, kind="ExternalOutput").ap()
    block_program(nc, *args, out)
    got = run_bass_kernel_spmd(nc, [arrays], core_ids=[0]).results[0]["result"]
    return got.reshape(1, SEQ, D)
```
